# Optimizing a Trainium2 kernel written in Bass

```python
import jax, jax.numpy as jnp
from jax import lax
import numpy as np

D_MODEL = 1024
BATCH = 1
SEQ = 256
DEPTH = 1

MIX_WIDTH = D_MODEL
CONV_CH = MIX_WIDTH // 2
RWKV_CH = MIX_WIDTH - CONV_CH
RWKV_HEAD = 64
RWKV_HEADS = RWKV_CH // RWKV_HEAD
CONV_WIDTH = 31
LORA_W = 64
LORA_A = 64
LORA_G = 128
RWKV_PROJ = 3 * RWKV_CH + LORA_W + LORA_A + LORA_G
IN_PROJ = 2 * CONV_CH + RWKV_PROJ
RWKV_SPLITS = [RWKV_CH, 2 * RWKV_CH, 3 * RWKV_CH, 3 * RWKV_CH + LORA_W, 3 * RWKV_CH + LORA_W + LORA_A]
PEER_HEADS = 8
PEER_NKEYS = 128
PEER_EXPERTS = PEER_NKEYS * PEER_NKEYS
PEER_DQ = 256
PEER_TOPK = 16
PEER_CHUNK = 128
RMS_EPS = 1e-6
LN_EPS = 1e-5
GN_EPS = 64e-5


F32 = jnp.float32

def rmsnorm(x, g):
    xf = x.astype(F32)
    y = xf * lax.rsqrt(jnp.mean(xf * xf, axis=-1, keepdims=True) + RMS_EPS)
    return (y * g.astype(F32)).astype(x.dtype)

def modulate(x, shift, scale):
    return x * (1 + scale[:, None, :]) + shift[:, None, :]

def conformer_conv(p_conv, w_dw, b_dw, ln_w, ln_b):
    a, b = jnp.split(p_conv, 2, axis=-1)
    y = a * jax.nn.sigmoid(b)
    y = lax.conv_general_dilated(
        y, w_dw[:, None, :], window_strides=(1,), padding=[(CONV_WIDTH - 1, 0)],
        dimension_numbers=('NWC', 'WIO', 'NWC'), feature_group_count=CONV_CH) + b_dw
    yf = y.astype(F32)
    mu = jnp.mean(yf, axis=-1, keepdims=True)
    var = jnp.mean(jnp.square(yf - mu), axis=-1, keepdims=True)
    yf = (yf - mu) * lax.rsqrt(var + LN_EPS) * ln_w.astype(F32) + ln_b.astype(F32)
    return jax.nn.silu(yf).astype(p_conv.dtype)

def token_shift(p, mu):
    prev = jnp.pad(p, ((0, 0), (1, 0), (0, 0)))[:, :-1]
    return p + mu * (prev - p)

def rwkv7_mix(p_rwkv, mu, w0, w2, a0, a2, g2, k_k, k_a, r_k, gn_w, gn_b):
    B, S, _ = p_rwkv.shape
    xs = token_shift(p_rwkv, mu)
    r, k, v, wl, al, gl = jnp.split(xs, RWKV_SPLITS, axis=-1)
    w = -jax.nn.softplus(-(w0 + jnp.tanh(wl) @ w2)) - 0.5
    decay = jnp.exp(-jnp.exp(w.astype(F32)))
    a = jax.nn.sigmoid(a0 + al @ a2)
    g = jax.nn.sigmoid(gl) @ g2
    kk = k * k_k
    k = k * (1 + (a - 1) * k_a)

    def heads(t):
        return t.reshape(B, S, RWKV_HEADS, RWKV_HEAD).astype(F32)

    kk_h = heads(kk)
    kk_h = kk_h / jnp.maximum(jnp.sqrt(jnp.sum(kk_h * kk_h, axis=-1, keepdims=True)), 1e-12)
    r_h, k_h, v_h, w_h, a_h = heads(r), heads(k), heads(v), decay.reshape(B, S, RWKV_HEADS, RWKV_HEAD), heads(a)

    def step(state, inp):
        r_t, k_t, v_t, w_t, kk_t, a_t = inp
        sa = jnp.einsum('bhij,bhj->bhi', state, -kk_t)
        state = (state * w_t[:, :, None, :]
                 + sa[..., None] * (kk_t * a_t)[:, :, None, :]
                 + v_t[..., None] * k_t[:, :, None, :])
        y_t = jnp.einsum('bhij,bhj->bhi', state, r_t)
        return state, y_t

    def seq_first(t):
        return jnp.moveaxis(t, 1, 0)

    state0 = jnp.zeros((B, RWKV_HEADS, RWKV_HEAD, RWKV_HEAD), F32)
    _, y = lax.scan(step, state0, (seq_first(r_h), seq_first(k_h), seq_first(v_h),
                                   seq_first(w_h), seq_first(kk_h), seq_first(a_h)))
    y = jnp.moveaxis(y, 0, 1)
    mean = jnp.mean(y, axis=-1, keepdims=True)
    var = jnp.mean(jnp.square(y - mean), axis=-1, keepdims=True)
    y = ((y - mean) * lax.rsqrt(var + GN_EPS)).reshape(B, S, RWKV_CH) * gn_w.astype(F32) + gn_b.astype(F32)
    bonus = jnp.sum(r_h * k_h * r_k.astype(F32), axis=-1, keepdims=True) * v_h
    y = y + bonus.reshape(B, S, RWKV_CH)
    return (y * g.astype(F32)).astype(p_rwkv.dtype)

def peer_ffn(u, w_q, sub_keys, expert_u, expert_v):
    B, S, D = u.shape
    tokens = u.reshape(-1, PEER_CHUNK, D)

    def chunk(xc):
        tc = xc.shape[0]
        q = (xc @ w_q).reshape(tc, PEER_HEADS, 2, PEER_DQ // 2)
        s = jnp.einsum('thpd,hpkd->thpk', q, sub_keys).astype(F32)
        s_top, i_top = lax.top_k(s, PEER_TOPK)
        cand = s_top[:, :, 0, :, None] + s_top[:, :, 1, None, :]
        cand_idx = i_top[:, :, 0, :, None] * PEER_NKEYS + i_top[:, :, 1, None, :]
        best, pos = lax.top_k(cand.reshape(tc, PEER_HEADS, PEER_TOPK * PEER_TOPK), PEER_TOPK)
        expert = jnp.take_along_axis(cand_idx.reshape(tc, PEER_HEADS, PEER_TOPK * PEER_TOPK), pos, axis=-1)
        gate = jax.nn.softmax(best, axis=-1)
        ue = jnp.take(expert_u, expert, axis=0)
        ve = jnp.take(expert_v, expert, axis=0)
        h = jax.nn.gelu(jnp.einsum('thkd,td->thk', ue, xc).astype(F32), approximate=False)
        return jnp.einsum('thk,thkd->td', (gate * h).astype(xc.dtype), ve)

    out = lax.map(chunk, tokens)
    return out.reshape(B, S, D)

def first_inputs(seed: int = 0) -> dict:
    key = jax.random.key(seed)
    ks = iter(jax.random.split(key, 32))

    def nrm(shape, scale):
        return scale * jax.random.normal(next(ks), shape, jnp.float32)

    def gain(shape):
        return 1.0 + nrm(shape, 0.02)

    L = DEPTH
    return {
        'x': nrm((BATCH, SEQ, D_MODEL), 1.0),
        'c': nrm((BATCH, D_MODEL), 1.0),
        'ada_w': nrm((L, D_MODEL, 6 * D_MODEL), D_MODEL ** -0.5),
        'ada_b': nrm((L, 6 * D_MODEL), 0.02),
        'norm_mix_g': gain((L, D_MODEL)),
        'w_in': nrm((L, D_MODEL, IN_PROJ), D_MODEL ** -0.5),
        'conv_dw_w': nrm((L, CONV_WIDTH, CONV_CH), CONV_WIDTH ** -0.5),
        'conv_dw_b': nrm((L, CONV_CH), 0.02),
        'conv_ln_w': gain((L, CONV_CH)),
        'conv_ln_b': nrm((L, CONV_CH), 0.02),
        'rwkv_mu': jax.random.uniform(next(ks), (L, RWKV_PROJ), jnp.float32),
        'rwkv_w0': jax.random.uniform(next(ks), (L, RWKV_CH), jnp.float32, -6.0, 1.0),
        'rwkv_w2': nrm((L, LORA_W, RWKV_CH), 0.5 * LORA_W ** -0.5),
        'rwkv_a0': nrm((L, RWKV_CH), 0.1),
        'rwkv_a2': nrm((L, LORA_A, RWKV_CH), 0.5 * LORA_A ** -0.5),
        'rwkv_g2': nrm((L, LORA_G, RWKV_CH), LORA_G ** -0.5),
        'rwkv_k_k': 0.85 + nrm((L, RWKV_CH), 0.02),
        'rwkv_k_a': gain((L, RWKV_CH)),
        'rwkv_r_k': nrm((L, RWKV_HEADS, RWKV_HEAD), 0.1),
        'rwkv_gn_w': gain((L, RWKV_CH)),
        'rwkv_gn_b': nrm((L, RWKV_CH), 0.02),
        'w_out': nrm((L, MIX_WIDTH, D_MODEL), MIX_WIDTH ** -0.5),
        'norm_ffn_g': gain((L, D_MODEL)),
        'peer_w_q': nrm((L, D_MODEL, PEER_HEADS * PEER_DQ), D_MODEL ** -0.5),
        'peer_sub_keys': nrm((L, PEER_HEADS, 2, PEER_NKEYS, PEER_DQ // 2), (PEER_DQ // 2) ** -0.5),
        'peer_u': nrm((L, PEER_EXPERTS, D_MODEL), D_MODEL ** -0.5),
        'peer_v': nrm((L, PEER_EXPERTS, D_MODEL), (PEER_HEADS * PEER_TOPK) ** -0.5),
        'final_g': gain((D_MODEL,)),
    }

def first_block(x, c, ada_w, ada_b, norm_mix_g, w_in, conv_dw_w, conv_dw_b, conv_ln_w, conv_ln_b,
              rwkv_mu, rwkv_w0, rwkv_w2, rwkv_a0, rwkv_a2, rwkv_g2, rwkv_k_k, rwkv_k_a, rwkv_r_k,
              rwkv_gn_w, rwkv_gn_b, w_out, norm_ffn_g, peer_w_q, peer_sub_keys, peer_u, peer_v, final_g):
    for l in range(DEPTH):
        mod = jax.nn.silu(c) @ ada_w[l] + ada_b[l]
        sh_mix, sc_mix, gt_mix, sh_ffn, sc_ffn, gt_ffn = jnp.split(mod, 6, axis=-1)

        u = modulate(rmsnorm(x, norm_mix_g[l]), sh_mix, sc_mix)
        p = u @ w_in[l]
        y_conv = conformer_conv(p[..., :2 * CONV_CH], conv_dw_w[l], conv_dw_b[l], conv_ln_w[l], conv_ln_b[l])
        y_rwkv = rwkv7_mix(p[..., 2 * CONV_CH:], rwkv_mu[l], rwkv_w0[l], rwkv_w2[l], rwkv_a0[l], rwkv_a2[l],
                           rwkv_g2[l], rwkv_k_k[l], rwkv_k_a[l], rwkv_r_k[l], rwkv_gn_w[l], rwkv_gn_b[l])
        mix = jnp.concatenate([y_conv, y_rwkv], axis=-1) @ w_out[l]
        x = x + gt_mix[:, None, :] * mix

        u = modulate(rmsnorm(x, norm_ffn_g[l]), sh_ffn, sc_ffn)
        x = x + gt_ffn[:, None, :] * peer_ffn(u, peer_w_q[l], peer_sub_keys[l], peer_u[l], peer_v[l])
    return rmsnorm(x, final_g)


HEAD_DIM = 128
DSA_HEADS = 4
MOBA_HEADS = 4
IDX_HEADS = 8
IDX_DIM = 64
DSA_TOPK_MAX = 256
MOBA_BLOCK = 256
MOBA_TOPK = 3
D_FF = -(-8 * D_MODEL // 768) * 256
ROPE_THETA = 10000.0
EPS = 1e-6
NEG = -1e30
DSA_Q_BLOCK = 128
MOBA_Q_BLOCK = 32
DSA_W = DSA_HEADS * HEAD_DIM
MOBA_W = MOBA_HEADS * HEAD_DIM
IN_SIZES = (DSA_W, DSA_W, DSA_W, IDX_HEADS * IDX_DIM, IDX_DIM, IDX_HEADS,
            MOBA_W, MOBA_W, MOBA_W, D_MODEL, D_MODEL)
IN_W = sum(IN_SIZES)
N_MOD = 6


def rms_norm(x, gain):
    xf = x.astype(jnp.float32)
    y = xf * lax.rsqrt(jnp.mean(xf * xf, axis=-1, keepdims=True) + EPS)
    return (y * gain.astype(jnp.float32)).astype(x.dtype)

def rope_tables(seq, dim):
    inv = ROPE_THETA ** (-jnp.arange(0, dim, 2, dtype=jnp.float32) / dim)
    ang = jnp.arange(seq, dtype=jnp.float32)[:, None] * inv[None, :]
    return jnp.cos(ang)[:, None, :], jnp.sin(ang)[:, None, :]

def apply_rope(x, cos, sin):
    x1, x2 = jnp.split(x.astype(jnp.float32), 2, axis=-1)
    return jnp.concatenate([x1 * cos - x2 * sin, x2 * cos + x1 * sin], axis=-1).astype(x.dtype)

def dsa_attention(q, k, v, qi, ki, wi):
    B, S, H, Dh = q.shape
    topk = min(DSA_TOPK_MAX, S // 4)
    nq = S // DSA_Q_BLOCK
    scale = Dh ** -0.5
    key_pos = jnp.arange(S)
    bi = jnp.arange(B)[:, None, None]

    def chunks(a):
        return jnp.moveaxis(a.reshape(a.shape[0], nq, DSA_Q_BLOCK, *a.shape[2:]), 1, 0)

    def block(args):
        qb, qib, wib, t = args
        logits = jnp.einsum('bqhd,bsd->bqhs', qib, ki).astype(jnp.float32)
        score = jnp.einsum('bqh,bqhs->bqs', wib.astype(jnp.float32), jax.nn.relu(logits))
        score = jnp.where((key_pos[None, :] <= t[:, None])[None], score, NEG)
        _, sel = lax.top_k(score, topk)
        ks = k[bi, sel]
        vs = v[bi, sel]
        s = jnp.einsum('bqhd,bqkhd->bhqk', qb, ks).astype(jnp.float32) * scale
        valid = sel <= t[None, :, None]
        s = jnp.where(valid[:, None], s, NEG)
        p = jax.nn.softmax(s, axis=-1).astype(v.dtype)
        return jnp.einsum('bhqk,bqkhd->bqhd', p, vs)

    t_c = jnp.arange(S).reshape(nq, DSA_Q_BLOCK)
    out = lax.map(block, (chunks(q), chunks(qi), chunks(wi), t_c))
    return jnp.moveaxis(out, 0, 1).reshape(B, S, H * Dh)

def moba_attention(q, k, v):
    B, S, H, Dh = q.shape
    nb = -(-S // MOBA_BLOCK)
    pad = nb * MOBA_BLOCK - S
    scale = Dh ** -0.5
    qh = q.transpose(0, 2, 1, 3)
    padw = ((0, 0), (0, 0), (0, pad), (0, 0))
    kh = jnp.pad(k.transpose(0, 2, 1, 3), padw).reshape(B, H, nb, MOBA_BLOCK, Dh)
    vh = jnp.pad(v.transpose(0, 2, 1, 3), padw).reshape(B, H, nb, MOBA_BLOCK, Dh)
    own = (jnp.arange(S) // MOBA_BLOCK).astype(jnp.int32)
    own_b = jnp.broadcast_to(own[:, None], (B, H, S, 1))
    n_sel = min(MOBA_TOPK, nb - 1)
    if n_sel > 0:
        kmean = jnp.mean(kh.astype(jnp.float32), axis=3)
        gate = jnp.einsum('bhsd,bhnd->bhsn', qh.astype(jnp.float32), kmean)
        past = jnp.arange(nb)[None, :] < own[:, None]
        gate = jnp.where(past, gate, NEG)
        _, sel = lax.top_k(gate, n_sel)
        blocks = jnp.concatenate([sel.astype(jnp.int32), own_b], axis=-1)
        bvalid = jnp.concatenate([sel < own[:, None], jnp.ones((B, H, S, 1), bool)], axis=-1)
    else:
        blocks = own_b
        bvalid = jnp.ones((B, H, S, 1), bool)
    nq = S // MOBA_Q_BLOCK
    bi = jnp.arange(B)[:, None, None, None]
    hi = jnp.arange(H)[None, :, None, None]
    offs = jnp.arange(MOBA_BLOCK)

    def chunks(a):
        return jnp.moveaxis(a.reshape(B, H, nq, MOBA_Q_BLOCK, *a.shape[3:]), 2, 0)

    def block(args):
        qb, bl, bv, t = args
        kg = kh[bi, hi, bl]
        vg = vh[bi, hi, bl]
        s = jnp.einsum('bhqd,bhqnkd->bhqnk', qb, kg).astype(jnp.float32) * scale
        kpos = bl[..., None] * MOBA_BLOCK + offs
        mask = bv[..., None] & (kpos <= t[:, None, None])
        s = jnp.where(mask, s, NEG)
        shp = s.shape
        p = jax.nn.softmax(s.reshape(shp[0], shp[1], shp[2], -1), axis=-1).reshape(shp).astype(v.dtype)
        return jnp.einsum('bhqnk,bhqnkd->bhqd', p, vg)

    t_c = jnp.arange(S).reshape(nq, MOBA_Q_BLOCK)
    out = lax.map(block, (chunks(qh), chunks(blocks), chunks(bvalid), t_c))
    out = jnp.moveaxis(out, 0, 2).reshape(B, H, S, Dh)
    return out.transpose(0, 2, 1, 3).reshape(B, S, H * Dh)

def second_inputs(seed: int = 0) -> dict:
    key = jax.random.key(seed)
    ks = jax.random.split(key, 16)
    f32 = jnp.float32

    def w(k, shape, fan_in):
        return jax.random.normal(k, shape, f32) * fan_in ** -0.5

    def gain(k, shape):
        return 1.0 + 0.02 * jax.random.normal(k, shape, f32)

    return {
        "x": jax.random.normal(ks[0], (BATCH, SEQ, D_MODEL), f32),
        "c": jax.random.normal(ks[1], (BATCH, D_MODEL), f32),
        "w_mod": w(ks[2], (DEPTH, D_MODEL, N_MOD * D_MODEL), D_MODEL),
        "b_mod": 0.02 * jax.random.normal(ks[3], (DEPTH, N_MOD * D_MODEL), f32),
        "g_mix_norm": gain(ks[4], (DEPTH, D_MODEL)),
        "g_ffn_norm": gain(ks[5], (DEPTH, D_MODEL)),
        "w_in": w(ks[6], (DEPTH, D_MODEL, IN_W), D_MODEL),
        "g_q_dsa": gain(ks[7], (DEPTH, HEAD_DIM)),
        "g_k_dsa": gain(ks[8], (DEPTH, HEAD_DIM)),
        "g_q_moba": gain(ks[9], (DEPTH, HEAD_DIM)),
        "g_k_moba": gain(ks[10], (DEPTH, HEAD_DIM)),
        "w_br_dsa": w(ks[11], (DEPTH, DSA_W, D_MODEL), DSA_W),
        "w_br_moba": w(ks[12], (DEPTH, MOBA_W, D_MODEL), MOBA_W),
        "w_out": w(ks[13], (DEPTH, D_MODEL, D_MODEL), D_MODEL),
        "w_gate_up": w(ks[14], (DEPTH, D_MODEL, 2 * D_FF), D_MODEL),
        "w_down": w(ks[15], (DEPTH, D_FF, D_MODEL), D_FF),
    }

def second_block(x, c, w_mod, b_mod, g_mix_norm, g_ffn_norm, w_in, g_q_dsa, g_k_dsa,
              g_q_moba, g_k_moba, w_br_dsa, w_br_moba, w_out, w_gate_up, w_down):
    B, S, _ = x.shape
    cos_h, sin_h = rope_tables(S, HEAD_DIM)
    cos_i, sin_i = rope_tables(S, IDX_DIM)
    split_at = np.cumsum(IN_SIZES)[:-1].tolist()
    idx_w_scale = (IDX_HEADS ** -0.5) * (IDX_DIM ** -0.5)
    for l in range(DEPTH):
        mod = jax.nn.silu(c) @ w_mod[l] + b_mod[l]
        sh_m, sc_m, gt_m, sh_f, sc_f, gt_f = [m[:, None, :] for m in jnp.split(mod, N_MOD, axis=-1)]

        h = rms_norm(x, g_mix_norm[l]) * (1.0 + sc_m) + sh_m
        proj = h @ w_in[l]
        (q_a, k_a, v_a, q_i, k_i, w_i, q_b, k_b, v_b, gate_a, gate_b) = jnp.split(proj, split_at, axis=-1)
        q_a = apply_rope(rms_norm(q_a.reshape(B, S, DSA_HEADS, HEAD_DIM), g_q_dsa[l]), cos_h, sin_h)
        k_a = apply_rope(rms_norm(k_a.reshape(B, S, DSA_HEADS, HEAD_DIM), g_k_dsa[l]), cos_h, sin_h)
        v_a = v_a.reshape(B, S, DSA_HEADS, HEAD_DIM)
        q_i = apply_rope(q_i.reshape(B, S, IDX_HEADS, IDX_DIM), cos_i, sin_i)
        k_i = apply_rope(k_i[:, :, None, :], cos_i, sin_i)[:, :, 0, :]
        w_i = w_i * idx_w_scale
        o_a = dsa_attention(q_a, k_a, v_a, q_i, k_i, w_i)

        q_b = apply_rope(rms_norm(q_b.reshape(B, S, MOBA_HEADS, HEAD_DIM), g_q_moba[l]), cos_h, sin_h)
        k_b = apply_rope(rms_norm(k_b.reshape(B, S, MOBA_HEADS, HEAD_DIM), g_k_moba[l]), cos_h, sin_h)
        v_b = v_b.reshape(B, S, MOBA_HEADS, HEAD_DIM)
        o_b = moba_attention(q_b, k_b, v_b)

        merged = (jax.nn.sigmoid(gate_a) * (o_a @ w_br_dsa[l])
                  + jax.nn.sigmoid(gate_b) * (o_b @ w_br_moba[l]))
        x = x + gt_m * (merged @ w_out[l])

        h = rms_norm(x, g_ffn_norm[l]) * (1.0 + sc_f) + sh_f
        g_ff, u_ff = jnp.split(h @ w_gate_up[l], 2, axis=-1)
        x = x + gt_f * ((jax.nn.silu(g_ff) * u_ff) @ w_down[l])
    return x


def setup_inputs(seed=0):
    out = dict(first_inputs(seed))
    for name, value in second_inputs(seed + 1).items():
        if name != "x":
            out[name + "_2"] = value
    return out


def reference(
    x, c, ada_w, ada_b, norm_mix_g, w_in, conv_dw_w, conv_dw_b, conv_ln_w, conv_ln_b, rwkv_mu,
    rwkv_w0, rwkv_w2, rwkv_a0, rwkv_a2, rwkv_g2, rwkv_k_k, rwkv_k_a, rwkv_r_k, rwkv_gn_w,
    rwkv_gn_b, w_out, norm_ffn_g, peer_w_q, peer_sub_keys, peer_u, peer_v, final_g, c_2,
    w_mod_2, b_mod_2, g_mix_norm_2, g_ffn_norm_2, w_in_2, g_q_dsa_2, g_k_dsa_2, g_q_moba_2,
    g_k_moba_2, w_br_dsa_2, w_br_moba_2, w_out_2, w_gate_up_2, w_down_2,
):
    x = first_block(
        x, c, ada_w, ada_b, norm_mix_g, w_in, conv_dw_w, conv_dw_b, conv_ln_w, conv_ln_b,
        rwkv_mu, rwkv_w0, rwkv_w2, rwkv_a0, rwkv_a2, rwkv_g2, rwkv_k_k, rwkv_k_a, rwkv_r_k,
        rwkv_gn_w, rwkv_gn_b, w_out, norm_ffn_g, peer_w_q, peer_sub_keys, peer_u, peer_v,
        final_g,
    )
    return second_block(
        x, c_2, w_mod_2, b_mod_2, g_mix_norm_2, g_ffn_norm_2, w_in_2, g_q_dsa_2, g_k_dsa_2,
        g_q_moba_2, g_k_moba_2, w_br_dsa_2, w_br_moba_2, w_out_2, w_gate_up_2, w_down_2,
    )


_drawn_inputs = setup_inputs


def setup_inputs(seed=0):
    import zlib

    import numpy as np

    out = dict(_drawn_inputs(seed))
    spreads = {}
    factors = {'norm_mix_g': 4.509,
     'conv_dw_b': 5.268,
     'conv_ln_w': 6.759,
     'conv_ln_b': 6.914,
     'rwkv_w2': 2.905,
     'rwkv_a0': 4.147,
     'rwkv_k_k': 3.416,
     'rwkv_k_a': 3.591,
     'rwkv_gn_w': 7.424,
     'rwkv_gn_b': 7.369,
     'norm_ffn_g': 8.0,
     'g_mix_norm_2': 5.077,
     'g_ffn_norm_2': 4.07,
     'g_q_dsa_2': 8.0,
     'g_k_dsa_2': 8.0,
     'g_q_moba_2': 8.0,
     'g_k_moba_2': 8.0}
    for name, (base, spread) in spreads.items():
        noise = np.random.default_rng([zlib.crc32(name.encode()), seed]).standard_normal(out[name].shape)
        drawn = base * np.exp(spread * noise) if base else spread * noise
        out[name] = __import__('jax').numpy.asarray(drawn.astype(out[name].dtype))
    for name, factor in factors.items():
        out[name] = (out[name] * factor).astype(out[name].dtype)
    return out
```

```python
from contextlib import ExitStack

import numpy as np
import concourse.bass as bass
from concourse import mybir

ALU = mybir.AluOpType
ACT = mybir.ActivationFunctionType
F32 = mybir.dt.float32
U32 = mybir.dt.uint32
AX_X = mybir.AxisListType.X

P = 128
D = 1024
KT = D // P
T = 256
TT = T // P
CH = 512
CT = CH // P
TAPS = 31
NPROJ = 14
C = 64
NC = T // C
HEADS, NKEYS, TOPK = 8, 128, 16
NSEL = HEADS * TOPK
DSA_TOPK = 64
FF = 2816
FT = FF // P
HD = 128
NEG = -1e30
TAKEN = -3e38
RMS_EPS, LN_EPS, GN_EPS = 1e-6, 1e-5, 64e-5
RING = 4
SLOT = KT * 512
GRING = 8

VECS = [("ada_b", 48), ("norm_mix_g", 8), ("conv_dw_w", TAPS * CT), ("conv_dw_b", CT), ("conv_ln_w", CT),
        ("conv_ln_b", CT), ("rwkv_mu", NPROJ), ("rwkv_w0", CT), ("rwkv_a0", CT), ("rwkv_k_k", CT),
        ("rwkv_k_a", CT), ("rwkv_r_k", CT), ("rwkv_gn_w", CT), ("rwkv_gn_b", CT), ("norm_ffn_g", 8),
        ("final_g", 8), ("c", 8), ("c_2", 8), ("b_mod_2", 48), ("g_mix_norm_2", 8), ("g_ffn_norm_2", 8),
        ("g_q_dsa_2", 1), ("g_k_dsa_2", 1), ("g_q_moba_2", 1), ("g_k_moba_2", 1)]
VCOL, _n = {}, 0
for _name, _w in VECS:
    VCOL[_name] = _n
    _n += _w
NVEC = _n

CONSTS = [("ident", P), ("ones", P), ("bones", P), ("dS", C), ("oS", C), ("mS", C), ("mI", C), ("dL", C),
          ("oL", C), ("eye", C), ("chunk", T), ("iota", TOPK)]
CCOL, _n = {}, 0
for _name, _w in CONSTS:
    CCOL[_name] = (_n, _w)
    _n += _w
NCONST = _n

SLOTS = {}
_n = 0
for _name, _w in [("ada", 12), ("w_in", 6), ("lora", 1), ("mod2", 12), ("w_out", 2), ("w_q", 4), ("keys", 1),
                  ("w_in2", 12), ("rope", 1), ("w_br", 2), ("w_out2", 2), ("w_gu", 11), ("w_down", 8)]:
    SLOTS[_name] = (_n, _w)
    _n += _w
NSLOTS = _n


def shape_constants():
    c = np.zeros((P, NCONST), np.float32)

    def put(name, a):
        o, w = CCOL[name]
        c[:, o:o + w] = a
    r = np.arange(P)[:, None] % C
    q = np.arange(C)[None, :]
    same = r // 16 == q // 16
    put("ident", np.eye(P))
    put("ones", 1.0)
    put("bones", np.arange(P)[:, None] // C == np.arange(P)[None, :] // C)
    put("dS", (r < q) & same)
    put("oS", (r < q) & ~same)
    put("mS", r < q)
    put("mI", r <= q)
    put("dL", (q < r) & same)
    put("oL", (q < r) & ~same)
    put("eye", r == q)
    put("chunk", np.arange(T)[None, :] % C != 0)
    put("iota", np.arange(TOPK)[None, :])

    rope = np.zeros((P, SLOT), np.float32)
    for n, dim in enumerate((HD, 64)):
        inv = 10000.0 ** (-np.arange(0, dim, 2, dtype=np.float32) / np.float32(dim))
        ang = (np.arange(T, dtype=np.float32)[:, None] * inv[None, :].astype(np.float32)).T
        reps = P // (dim // 2)
        rope[:, n * 512:n * 512 + T] = np.tile(np.cos(ang), (reps, 1))
        rope[:, n * 512 + T:n * 512 + 512] = np.tile(np.sin(ang), (reps, 1))
        rot = np.zeros((P, P), np.float32)
        for i in range(P):
            if i % dim < dim // 2:
                rot[i + dim // 2, i] = -1.0
            else:
                rot[i - dim // 2, i] = 1.0
        rope[:, 1536 + n * P:1536 + (n + 1) * P] = rot
    t = np.arange(TT)[None, :, None] * P + np.arange(P)[:, None, None]
    rope[:, 1024:1536] = np.where(np.arange(T)[None, None, :] <= t, 0.0, NEG).reshape(P, 512)
    return c, rope


def build(nc, xT_in, vecs_in, consts_in, slots_in, experts_in, out):
    with ExitStack() as ctx:
        def sb(name, shape, dt=F32):
            return ctx.enter_context(nc.sbuf_tensor(name, shape, dt))

        def sem(name):
            return ctx.enter_context(nc.semaphore(name))

        psum = [ctx.enter_context(nc.psum_tensor(f"bank{i}", [P, 512], F32)) for i in range(8)]
        ring = sb("ring", [P, RING, SLOT])
        xT = sb("xT", [P, KT, T])
        uT = sb("uT", [P, KT, T])
        mixT = sb("mixT", [P, KT, T])
        vec = sb("vec", [P, NVEC])
        con = sb("con", [P, NCONST])
        mod1 = sb("mod1", [P, 48])
        mod2 = sb("mod2", [P, 48])
        gain = sb("gain", [P, 4, KT])
        csil = sb("csil", [P, 2, KT])
        rstd = sb("rstd", [P, T])
        epsc = sb("epsc", [P, 4])
        ARENA = 28500
        arena = sb("arena", [P, ARENA])

        def area(at, *shape):
            n = int(np.prod(shape))
            assert at + n <= ARENA, (at, shape)
            a = arena[:, at:at + n]
            if len(shape) == 1:
                return a
            names = "abcde"[:len(shape)]
            kw = {k: s for k, s in zip(names[1:], shape[1:])}
            return a.rearrange(f"p ({' '.join(names)}) -> p {' '.join(names)}", **kw)

        def cst(name):
            o, w = CCOL[name]
            return con[:, o:o + w]

        def vcol(name, j=0, n=1):
            return vec[:, VCOL[name] + j:VCOL[name] + j + n]

        ident, ones, bones = cst("ident"), cst("ones"), cst("bones")
        slot_loaded = [sem(f"slot_loaded{i}") for i in range(RING)]
        slot_used = [sem(f"slot_used{i}") for i in range(RING)]

        def slot(n, width=512, kts=KT):
            return ring[:, n % RING, 0:kts * width].rearrange("p (k n) -> p k n", k=kts)

        def wait_slot(eng, n):
            eng.wait_ge(slot_loaded[n % RING], 16 * (n // RING + 1))

        def free_slot(ins, n):
            ins.then_inc(slot_used[n % RING], 1)

        def load_slots(eng, first, last):
            for n in range(first, min(last, NSLOTS)):
                if n >= RING:
                    eng.wait_ge(slot_used[n % RING], n // RING)
                eng.dma_start(ring[:, n % RING, :], slots_in[n]).then_inc(slot_loaded[n % RING], 16)

        def after(name, part=None):
            o, w = SLOTS[name]
            return o + (w if part is None else part) + RING

        def done(eng, ins, s, value):
            ins.then_inc(s, 1)
            eng.wait_ge(s, value)

        class Chain:

            def __init__(self, eng, s):
                self.eng, self.s, self.n = eng, s, 0

            def __call__(self, ins):
                self.n += 1
                done(self.eng, ins, self.s, self.n)

        seq_v, seq_a, seq_g = sem("seq_v"), sem("seq_a"), sem("seq_g")
        chains = {}

        def chain(key, eng, s):
            if key not in chains:
                chains[key] = Chain(eng, s)
            chains[key].eng = eng
            return chains[key]

        def pe_modulation(pe, name, cs, bank, w_ready, part=None):
            s0, n = SLOTS[name]
            for s in range(n) if part is None else part:
                wait_slot(pe, s0 + s)
                for m in range(4):
                    col = 4 * s + m
                    for k in range(KT):
                        ins = pe.matmul(psum[bank][:, col:col + 1], slot(s0 + s)[:, k, m * P:(m + 1) * P],
                                        cs[:, k:k + 1], start=(k == 0), stop=(k == KT - 1))
                if s == n - 1:
                    ins.then_inc(w_ready, 1)
                else:
                    free_slot(ins, s0 + s)

        c_ready, mod1_mm, mod1_ready, in_ready = sem("c_ready"), sem("mod1_mm"), sem("mod1_ready"), sem("in_ready")
        with nc.Block() as block:
            @block.sync
            def _(sp):
                sp.dma_start(vec[:], vecs_in).then_inc(in_ready, 16)
                sp.dma_start(con[:], consts_in).then_inc(in_ready, 16)
                sp.dma_start(xT[:], xT_in).then_inc(in_ready, 16)
                load_slots(sp, 0, after("ada"))

            @block.scalar
            def _(act):
                act.wait_ge(in_ready, 48)
                act.activation(csil[:, 0, :], vcol("c", 0, 8), ACT.Silu).then_inc(c_ready, 1)
                act.activation(csil[:, 1, :], vcol("c_2", 0, 8), ACT.Silu).then_inc(c_ready, 1)

            @block.tensor
            def _(pe):
                pe.wait_ge(c_ready, 2)
                pe_modulation(pe, "ada", csil[:, 0, :], 0, mod1_mm)

            @block.vector
            def _(dve):
                v = chain("v", dve, seq_v)
                for j, e in enumerate((RMS_EPS, LN_EPS, GN_EPS, 1.0)):
                    v(dve.memset(epsc[:, j:j + 1], e))
                dve.wait_ge(in_ready, 48)
                dve.wait_ge(mod1_mm, 1)
                o, w = SLOTS["ada"]
                ins = dve.tensor_tensor(mod1[:], psum[0][:, 0:48], vcol("ada_b", 0, 48), ALU.add)
                free_slot(ins, o + w - 1)
                dve.wait_ge(slot_used[(o + w - 1) % RING], (o + w - 1) // RING + 1)
                for j, (g, sc) in enumerate((("norm_mix_g", 8), ("norm_ffn_g", 32))):
                    v(dve.scalar_tensor_tensor(gain[:, j, :], mod1[:, sc:sc + 8], 1.0, vcol(g, 0, 8),
                                               ALU.add, ALU.mult))
        if STOP == "mod":
            return

        def norm_block(tag, gains, shifts, dst, then_load=None):
            sq_ready, ms_ready, sd_ready, n_ready = (sem(f"{tag}_{x}") for x in ("sq", "ms", "sd", "n"))
            sq = dst
            with nc.Block() as block:
                @block.scalar
                def _(act):
                    act.activation(sq[:, :, :], xT[:, :, :], ACT.Square).then_inc(sq_ready, 1)
                    act.wait_ge(ms_ready, 1)
                    act.activation(rstd[:], psum[0][:, 0:T], ACT.Sqrt, bias=epsc[:, 0:1],
                                   scale=1.0 / D).then_inc(sd_ready, 1)

                @block.tensor
                def _(pe):
                    pe.wait_ge(sq_ready, 1)
                    for k in range(KT):
                        ins = pe.matmul(psum[0][:, 0:T], ones, sq[:, k, :], start=(k == 0), stop=(k == KT - 1))
                    ins.then_inc(ms_ready, 1)

                @block.vector
                def _(dve):
                    v = chain("v", dve, seq_v)
                    dve.wait_ge(sd_ready, 1)
                    v(dve.reciprocal(rstd[:], rstd[:]))
                    for k in range(KT):
                        ins = dve.scalar_tensor_tensor(dst[:, k, :], xT[:, k, :], gains[:, k:k + 1], rstd[:],
                                                       ALU.mult, ALU.mult).then_inc(n_ready, 1)
                    if shifts is not None:
                        for k in range(KT):
                            dve.wait_ge(n_ready, k + 1)
                            dve.tensor_scalar(dst[:, k, :], dst[:, k, :], shifts[:, k:k + 1], None, ALU.add)

        norm_block("mix", gain[:, 0, :], mod1[:, 0:8], uT)
        if STOP == "norm1":
            return

        pB = area(0, NPROJ, T + 1)
        xs = area(3598, NPROJ, T)
        ypad = area(7182, CT, TAPS - 1 + T)

        def pe_project(pe, name, tiles, rhs, mm, ev, base=0, banks=8, width=512, kts=KT, sl=None):
            s0, _ = SLOTS[name]
            for i, (s, col) in enumerate(tiles):
                if i == 0 or tiles[i - 1][0] != s:
                    wait_slot(pe, s0 + s)
                if i >= banks:
                    pe.wait_ge(ev, i - banks + 1)
                for k in range(kts):
                    ins = pe.matmul(psum[base + i % banks][:, 0:T], slot(s0 + s, width, kts)[:, k, col:col + P],
                                    rhs[:, k, :], start=(k == 0), stop=(k == kts - 1))
                ins.then_inc(mm, 1)

        in_mm, in_ev, in_sig, in_zero = sem("in_mm"), sem("in_ev"), sem("in_sig"), sem("in_zero")
        w_in_tiles = [(i // 4, (i % 4) * P) for i in range(22)]
        with nc.Block() as block:
            @block.sync
            def _(sp):
                load_slots(sp, after("ada"), after("w_in"))

            @block.gpsimd
            def _(pool):
                pool.memset(pB[:, :, 0:1], 0.0).then_inc(in_zero, 1)
                pool.memset(ypad[:, :, 0:TAPS - 1], 0.0).then_inc(in_zero, 1)

            @block.tensor
            def _(pe):
                pe_project(pe, "w_in", w_in_tiles, uT, in_mm, in_ev)

            @block.scalar
            def _(act):
                s0 = SLOTS["w_in"][0]
                for i in range(22):
                    act.wait_ge(in_mm, i + 1)
                    src = psum[i % 8][:, 0:T]
                    if i < 4:
                        ins = act.copy(ypad[:, i, TAPS - 1:], src)
                    elif i < 8:
                        ins = act.activation(mixT[:, i - 4, :], src, ACT.Sigmoid)
                    else:
                        ins = act.copy(pB[:, i - 8, 1:], src)
                    ins.then_inc(in_ev, 1)
                    if i % 4 == 3 or i == 21:
                        act.wait_ge(in_ev, i + 1)
                        act.sem_inc(slot_used[(s0 + i // 4) % RING], 1)

            @block.vector
            def _(dve):
                for i in range(4):
                    dve.wait_ge(in_ev, 5 + i)
                    dve.tensor_tensor(ypad[:, i, TAPS - 1:], ypad[:, i, TAPS - 1:], mixT[:, i, :], ALU.mult)
        if STOP == "w_in":
            return

        sqc = area(8960, CT, T)
        mean, var = area(9984, T), area(10240, T)
        cv_acc, cv_sq, cv_mm, cv_var, cv_sd, cv_out = (sem(f"cv_{x}") for x in ("acc", "sq", "mm", "var", "sd", "out"))
        with nc.Block() as block:
            @block.vector
            def _(dve):
                v = chain("v", dve, seq_v)
                for j in range(TAPS):
                    for ct in range(CT):
                        n = j * CT + ct
                        if j:
                            dve.wait_ge(cv_acc, n - CT + 1)
                        src, wc = ypad[:, ct, j:j + T], vcol("conv_dw_w", n)
                        if j == 0:
                            ins = dve.tensor_scalar(mixT[:, ct, :], src, wc, vcol("conv_dw_b", ct), ALU.mult, ALU.add)
                        else:
                            ins = dve.scalar_tensor_tensor(mixT[:, ct, :], src, wc, mixT[:, ct, :], ALU.mult, ALU.add)
                        ins.then_inc(cv_acc, 1)
                dve.wait_ge(cv_mm, 1)
                v(dve.tensor_scalar(mean, psum[0][:, 0:T], 1.0 / CH, None, ALU.mult))
                for ct in range(CT):
                    ins = dve.tensor_tensor(mixT[:, ct, :], mixT[:, ct, :], mean, ALU.subtract).then_inc(cv_acc, 1)
                dve.wait_ge(cv_sd, 1)
                v(dve.reciprocal(var, var))
                for ct in range(CT):
                    dve.wait_ge(cv_acc, TAPS * CT + ct + 1)
                    v(dve.scalar_tensor_tensor(mixT[:, ct, :], mixT[:, ct, :], vcol("conv_ln_w", ct), var,
                                               ALU.mult, ALU.mult))
                    dve.tensor_scalar(mixT[:, ct, :], mixT[:, ct, :], vcol("conv_ln_b", ct), None,
                                      ALU.add).then_inc(cv_out, 1)

            @block.tensor
            def _(pe):
                pe.wait_ge(cv_acc, TAPS * CT)
                for ct in range(CT):
                    ins = pe.matmul(psum[0][:, 0:T], ones, mixT[:, ct, :], start=(ct == 0), stop=(ct == CT - 1))
                ins.then_inc(cv_mm, 1)
                pe.wait_ge(cv_sq, 1)
                for ct in range(CT):
                    ins = pe.matmul(psum[1][:, 0:T], ones, sqc[:, ct, :], start=(ct == 0), stop=(ct == CT - 1))
                ins.then_inc(cv_mm, 1)

            @block.scalar
            def _(act):
                act.wait_ge(cv_acc, TAPS * CT + CT)
                act.activation(sqc, mixT[:, 0:CT, :], ACT.Square).then_inc(cv_sq, 1)
                act.wait_ge(cv_mm, 2)
                act.activation(var, psum[1][:, 0:T], ACT.Sqrt, bias=epsc[:, 1:2], scale=1.0 / CH).then_inc(cv_sd, 1)
                act.wait_ge(cv_out, CT)
                act.activation(mixT[:, 0:CT, :], mixT[:, 0:CT, :], ACT.Silu).then_inc(seq_a, 1)
        if STOP == "conv":
            return

        B0 = 8960
        BDk, BDb, BDc, BDr, BDv = (area(B0 + i * 2048, CT, NC, 2, C) for i in range(5))
        RH = area(B0 + 10240, CT, NC, 2, C)
        bS = area(B0 + 12288, CT, NC, C)
        gate = area(B0 + 13312, CT, T)
        bv = area(B0 + 14336, CT, T)
        dec = area(B0 + 15360, CT, NC, C + 1)
        T0 = area(B0 + 16400, CT, T)
        T1 = area(B0 + 17424, CT, T)
        T2, T3, T4 = uT[:, 0:4, :], uT[:, 4:8, :], mixT[:, 4:8, :]
        th = area(B0 + 18448, T)
        sg = area(B0 + 18704, T)
        assert B0 + 18960 <= ARENA

        def by_chunk(a):
            return a.rearrange("p c (n t) -> p c n t", n=NC)

        rw = {x: sem("rw_" + x) for x in ("zero", "xs", "th", "sg", "lora", "sigw", "a", "g", "ld", "L", "D", "sq",
                                          "ss", "nrm", "kap", "bs", "ks", "rs", "rk", "bonus", "bd", "k2")}
        with nc.Block() as block:
            @block.sync
            def _(sp):
                load_slots(sp, after("w_in"), after("lora"))

            @block.gpsimd
            def _(pool):
                g = chain("g", pool, seq_g)
                for b in (BDk, BDb, BDc, BDr, BDv):
                    g(pool.memset(b[0:64, :, :, 1, :], 0.0))
                    g(pool.memset(b[64:128, :, :, 0, :], 0.0))
                pool.memset(dec[:, :, :, 0:1], 1.0).then_inc(rw["zero"], 1)
                pool.wait_ge(rw["xs"], NPROJ)
                for hh in range(2):
                    s = slice(64 * hh, 64 * hh + 64)
                    g(pool.tensor_copy(BDv[s, :, :, hh, :], by_chunk(xs[s, 8:12, :])))

            @block.vector
            def _(dve):
                v = chain("v", dve, seq_v)
                v(dve.tensor_tensor(xs, pB[:, :, 0:T], pB[:, :, 1:T + 1], ALU.subtract))
                for i in (12, 13, *range(12)):
                    dve.scalar_tensor_tensor(xs[:, i, :], xs[:, i, :], vcol("rwkv_mu", i), pB[:, i, 1:T + 1],
                                             ALU.mult, ALU.add).then_inc(rw["xs"], 1)
                dve.wait_ge(rw["xs"], NPROJ)
                r, k = xs[:, 0:4, :], xs[:, 4:8, :]
                for ct in range(CT):
                    ins = dve.tensor_scalar(T4[:, ct, :], k[:, ct, :], vcol("rwkv_k_k", ct), None, ALU.mult)
                    v(ins)
                dve.tensor_tensor(bv, T4, T4, ALU.mult).then_inc(rw["sq"], 1)
                dve.wait_ge(rw["sigw"], CT)
                v(dve.tensor_scalar(T2, T0, -float(np.exp(np.float64(-0.5))), None, ALU.mult))
                for ct in range(CT):
                    dve.tensor_tensor_scan(T3[:, ct, :], cst("chunk"), T2[:, ct, :], 0.0, ALU.mult,
                                           ALU.add).then_inc(rw["L"], 1)
                dve.wait_ge(rw["a"], CT)
                dve.wait_ge(rw["L"], CT)
                for ct in range(CT):
                    v(dve.tensor_scalar(T0[:, ct, :], T1[:, ct, :], -1.0, vcol("rwkv_k_a", ct), ALU.add, ALU.mult))
                v(dve.scalar_tensor_tensor(T0, T0, 1.0, k, ALU.add, ALU.mult))
                for ct in range(CT):
                    v(dve.tensor_scalar(T2[:, ct, :], r[:, ct, :], vcol("rwkv_r_k", ct), None, ALU.mult))
                dve.tensor_tensor(T2, T2, T0, ALU.mult).then_inc(rw["rk"], 1)
                dve.wait_ge(rw["nrm"], 2)
                v(dve.tensor_scalar(bv, bv, 1e-12, None, ALU.max))
                v(dve.reciprocal(bv, bv))
                v(dve.tensor_tensor(T4, T4, bv, ALU.mult))
                v(dve.tensor_tensor(T1, T1, T4, ALU.mult))
                dve.wait_ge(rw["D"], CT)
                dve.wait_ge(rw["zero"], 1)
                v(dve.reciprocal(by_chunk(T3), dec[:, :, :, 1:]))
                for ct in range(CT):
                    dve.tensor_tensor(RH[:, ct, :, 0, :], by_chunk(T4)[:, ct], dec[:, ct, :, 0:C], ALU.mult).then_inc(rw["kap"], 1)
                    dve.tensor_tensor(RH[:, ct, :, 1, :], by_chunk(r)[:, ct], dec[:, ct, :, 1:], ALU.mult).then_inc(rw["rs"], 1)
                dve.tensor_tensor(bS.rearrange("p a b c -> p a (b c)"), T1, T3, ALU.mult).then_inc(rw["bs"], 1)
                v(dve.tensor_tensor(T0, T0, T3, ALU.mult))
                for hh in range(2):
                    s = slice(64 * hh, 64 * hh + 64)
                    dve.tensor_copy(BDk[s, :, :, hh, :], by_chunk(T0[s]))
                dve.wait_ge(rw["bonus"], 2)
                for h in range(2):
                    dve.tensor_tensor(bv[:, 2 * h:2 * h + 2, :], psum[6 + h][:, :].rearrange("p (c t) -> p c t", c=2),
                                      xs[:, 8 + 2 * h:10 + 2 * h, :], ALU.mult)

            @block.scalar
            def _(act):
                act.wait_ge(rw["xs"], 2)
                act.activation(th[0:64], xs[0:64, 12, :], ACT.Tanh).then_inc(rw["th"], 1)
                act.activation(sg, xs[:, 13, :], ACT.Sigmoid).then_inc(rw["sg"], 1)
                for ct in range(CT):
                    act.wait_ge(rw["lora"], ct // 2 * 2 + 2)
                    col = slice((ct % 2) * T, (ct % 2 + 1) * T)
                    act.activation(T0[:, ct, :], psum[ct // 2][:, col], ACT.Sigmoid,
                                   bias=vcol("rwkv_w0", ct)).then_inc(rw["sigw"], 1)
                    act.activation(T1[:, ct, :], psum[2 + ct // 2][:, col], ACT.Sigmoid,
                                   bias=vcol("rwkv_a0", ct)).then_inc(rw["a"], 1)
                    act.copy(gate[:, ct, :], psum[4 + ct // 2][:, col]).then_inc(rw["g"], 1)
                act.wait_ge(rw["zero"], 1)
                for ct in range(CT):
                    act.wait_ge(rw["L"], ct + 1)
                    act.activation(dec[:, ct, :, 1:], by_chunk(T3)[:, ct], ACT.Exp).then_inc(rw["D"], 1)
                for h in range(2):
                    act.wait_ge(rw["ss"], h + 1)
                    act.activation(bv[:, 2 * h:2 * h + 2, :], psum[6 + h][:, :].rearrange("p (c t) -> p c t", c=2),
                                   ACT.Sqrt).then_inc(rw["nrm"], 1)
                act.wait_ge(rw["kap"], CT)
                act.wait_ge(rw["rs"], CT)
                act.wait_ge(rw["bs"], 1)
                for hh in range(2):
                    s = slice(64 * hh, 64 * hh + 64)
                    act.copy(BDc[s, :, :, hh, :], RH[s, :, :, 0, :])
                    act.copy(BDr[s, :, :, hh, :], RH[s, :, :, 1, :])
                    act.copy(BDb[s, :, :, hh, :], bS[s])

            @block.tensor
            def _(pe):
                n = SLOTS["lora"][0]
                wait_slot(pe, n)
                lora = ring[:, n % RING, :]
                pe.wait_ge(rw["th"], 1)
                pe.wait_ge(rw["sg"], 1)
                for ct in range(CT):
                    col = slice((ct % 2) * T, (ct % 2 + 1) * T)
                    wc = slice(ct * P, ct * P + P)
                    pe.matmul(psum[ct // 2][:, col], lora[0:64, wc], th[0:64], start=True, stop=True)
                    pe.matmul(psum[2 + ct // 2][:, col], lora[64:128, wc], xs[64:128, 12, :], start=True, stop=True)
                    pe.matmul(psum[4 + ct // 2][:, col], lora[:, CH + ct * P:CH + ct * P + P], sg, start=True,
                              stop=True).then_inc(rw["lora"], 1)
                pe.wait_ge(rw["lora"], CT)
                pe.sem_inc(slot_used[n % RING], 1)
                pe.wait_ge(rw["sq"], 1)
                for ct in range(CT):
                    col = slice((ct % 2) * T, (ct % 2 + 1) * T)
                    ins = pe.matmul(psum[6 + ct // 2][:, col], bones, bv[:, ct, :], start=True, stop=True)
                    if ct % 2:
                        ins.then_inc(rw["ss"], 1)
                pe.wait_ge(rw["rk"], 1)
                pe.wait_ge(rw["nrm"], 2)
                for ct in range(CT):
                    col = slice((ct % 2) * T, (ct % 2 + 1) * T)
                    ins = pe.matmul(psum[6 + ct // 2][:, col], bones, T2[:, ct, :], start=True, stop=True)
                    if ct % 2:
                        ins.then_inc(rw["bonus"], 1)
        if STOP == "prep":
            return

        def bdm(at):
            return area(at, CT, P)
        names = ["Pd", "Po", "Md", "P2", "M2", "R0", "W0", "R1", "W1", "Q", "QT", "N", "RB", "RK", "tb", "tk"]
        mat = {n: bdm(i * 512) for i, n in enumerate(names)}
        Vs = area(8192, CT, C)
        Us = area(8448, CT, C)
        Ss = area(8704, CT, C)
        Rn = area(B0 + 17424, CT, C)
        yT = T0
        Ybd = uT[:, 0:2, :].rearrange("p a (c x) -> p (a c) x", c=2)
        yn = uT[:, 2:3, :].rearrange("p a (c x) -> p (a c) x", c=4)
        sq = uT[:, 3:4, :].rearrange("p a (c x) -> p (a c) x", c=4)
        st = area(B0 + 17680, 16)
        mod2_mm = sem("mod2_mm")
        rc_mm, rc_ev, rc_zero, rc_var, rc_sd = (sem(f"rc_{x}") for x in ("mm", "ev", "zero", "var", "sd"))

        def pairs(bank, n=P):
            return psum[bank][:, 0:CT * n].rearrange("p (c x) -> p c x", c=CT)

        class Steps:
            G1, G2, G3, TB, TK, TV, P2, M2, RA, WA, P4, M4, RB_, WB, P8, M8, RC, WC, Q_, QT_, Q2T, A_, Y_, RN, U_, S_, Y, YT = range(28)
            COUNT = 28
        S = Steps
        NEEDS = {S.P2: S.G3, S.M2: S.G3, S.RA: S.M2, S.WA: S.P2, S.P4: S.M2, S.M4: S.M2, S.RB_: S.M4, S.WB: S.P4,
                 S.P8: S.M4, S.M8: S.M4, S.RC: S.M8, S.WC: S.P8, S.Q_: S.WC, S.QT_: S.RC, S.Q2T: S.QT_, S.A_: S.Q2T,
                 S.Y_: S.A_, S.RN: S.TV, S.U_: S.RN, S.S_: S.U_, S.Y: S.U_, S.YT: S.Y}
        with nc.Block() as block:
            @block.sync
            def _(sp):
                load_slots(sp, after("lora"), after("mod2"))

            @block.gpsimd
            def _(pool):
                g = chain("g", pool, seq_g)
                for n in names:
                    if n not in ("tb", "tk"):
                        g(pool.memset(mat[n][0:64, :, C:P], 0.0))
                        g(pool.memset(mat[n][64:128, :, 0:C], 0.0))
                g(pool.memset(Ybd, 0.0))
                pool.memset(Ss, 0.0).then_inc(rc_zero, 1)

            @block.tensor
            def _(pe):
                pe.wait_ge(rc_zero, 1)
                for c in range(NC):
                    base = c * S.COUNT

                    def begin(k):
                        n = base + k
                        need = max(n - 6, base + NEEDS[k] + 1 if k in NEEDS else 0, 0)
                        if need > 0:
                            pe.wait_ge(rc_ev, need)
                        return n % 7

                    def products(k, terms, n=P, transpose=False):
                        b = begin(k)
                        for ct in range(CT):
                            for i, (l, r_) in enumerate(terms):
                                ins = pe.matmul(psum[b][:, ct * n:(ct + 1) * n], l(ct), r_(ct), start=(i == 0),
                                                stop=(i == len(terms) - 1))
                        ins.then_inc(rc_mm, 1)

                    def flip(k, src):
                        b = begin(k)
                        for ct in range(CT):
                            ins = pe.transpose(psum[b][:, ct * P:(ct + 1) * P], src(ct), ident)
                        ins.then_inc(rc_mm, 1)

                    def bd(a):
                        return lambda ct: a[:, ct, c].rearrange("p h t -> p (h t)")

                    def m(name):
                        return lambda ct: mat[name][:, ct, :]

                    def rh(lo, hi):
                        return lambda ct: RH[:, ct, c, lo:hi, :].rearrange("p a t -> p (a t)")
                    products(S.G1, [(bd(BDb), rh(0, 2))])
                    products(S.G2, [(bd(BDk), rh(0, 2))])
                    products(S.G3, [(bd(BDc), lambda ct: bS[:, ct, c, :])], C)
                    flip(S.TB, bd(BDb))
                    flip(S.TK, bd(BDk))
                    flip(S.TV, bd(BDv))
                    pe_modulation(pe, "mod2", csil[:, 1, :], 7, mod2_mm, [3 * c])
                    products(S.P2, [(m("Md"), m("Pd"))])
                    products(S.M2, [(m("Pd"), m("Md"))])
                    products(S.RA, [(m("M2"), m("R0"))])
                    products(S.WA, [(m("P2"), m("W0"))])
                    products(S.P4, [(m("M2"), m("P2"))])
                    products(S.M4, [(m("P2"), m("M2"))])
                    products(S.RB_, [(m("Md"), m("R1"))])
                    products(S.WB, [(m("Pd"), m("W1"))])
                    pe_modulation(pe, "mod2", csil[:, 1, :], 7, mod2_mm, [3 * c + 1])
                    products(S.P8, [(m("Md"), m("Pd"))])
                    products(S.M8, [(m("Pd"), m("Md"))])
                    products(S.RC, [(m("M2"), m("R0"))])
                    products(S.WC, [(m("P2"), m("W0"))])
                    products(S.Q_, [(m("W1"), m("Po"))])
                    products(S.QT_, [(m("Po"), m("W1"))])
                    products(S.Q2T, [(m("Q"), m("QT"))])
                    products(S.A_, [(m("P2"), m("R1"))])
                    products(S.Y_, [(m("QT"), m("R0"))])
                    products(S.RN, [(bd(BDc), lambda ct: Ss[:, ct, :]), (m("N"), lambda ct: Vs[:, ct, :])], C)
                    products(S.U_, [(m("R1"), lambda ct: Rn[:, ct, :])], C)
                    products(S.S_, [(m("tb"), lambda ct: Us[:, ct, :]), (m("tk"), lambda ct: Vs[:, ct, :])], C)
                    products(S.Y, [(bd(BDr), lambda ct: Ss[:, ct, :]), (m("RB"), lambda ct: Us[:, ct, :]),
                                   (m("RK"), lambda ct: Vs[:, ct, :])], C)
                    pe_modulation(pe, "mod2", csil[:, 1, :], 7, mod2_mm, [3 * c + 2])
                    flip(S.YT, lambda ct: Ybd[:, ct, :])

            @block.vector
            def _(dve):
                v = chain("v", dve, seq_v)
                dve.wait_ge(rc_zero, 1)
                ev = 0
                H = (slice(0, 64), slice(64, 128))
                for c in range(NC):
                    base = c * S.COUNT

                    def begin(k):
                        dve.wait_ge(rc_mm, base + k + 1)
                        return (base + k) % 7

                    def masked(dst, bank, half, mask, width=P, off=0):
                        s = H[half]
                        return dve.tensor_tensor(dst[s, :, half * C:half * C + C], pairs(bank, width)[s, :, off:off + C],
                                                 cst(mask)[s].unsqueeze(1).to_broadcast([64, CT, C]), ALU.mult)

                    def last(ins):
                        ins.then_inc(rc_ev, 1)

                    def copy(k, dst):
                        last(dve.tensor_copy(dst, pairs(begin(k))))

                    def combine(k, dst, a, op):
                        last(dve.tensor_tensor(dst, a, pairs(begin(k)), op))

                    b = begin(S.G1)
                    for h in range(2):
                        masked(mat["Po"], b, h, "oS")
                        masked(mat["RB"], b, h, "mI", off=C)
                        v(masked(mat["Pd"], b, h, "dS"))
                        s = H[h]
                        ins = dve.tensor_tensor(mat["R0"][s, :, h * C:h * C + C],
                                                cst("eye")[s].unsqueeze(1).to_broadcast([64, CT, C]),
                                                mat["Pd"][s, :, h * C:h * C + C], ALU.subtract)
                    last(ins)
                    b = begin(S.G2)
                    for h in range(2):
                        masked(mat["RK"], b, h, "mI", off=C)
                        ins = masked(mat["N"], b, h, "mS")
                    last(ins)
                    b = begin(S.G3)
                    for h in range(2):
                        v(masked(mat["Md"], b, h, "dL", width=C))
                        s = H[h]
                        ins = dve.tensor_tensor(mat["W0"][s, :, h * C:h * C + C],
                                                cst("eye")[s].unsqueeze(1).to_broadcast([64, CT, C]),
                                                mat["Md"][s, :, h * C:h * C + C], ALU.subtract)
                    last(ins)
                    copy(S.TB, mat["tb"])
                    copy(S.TK, mat["tk"])
                    b = begin(S.TV)
                    for h in range(2):
                        ins = dve.tensor_copy(Vs[H[h]], pairs(b)[H[h], :, h * C:h * C + C])
                    last(ins)
                    copy(S.P2, mat["P2"])
                    copy(S.M2, mat["M2"])
                    combine(S.RA, mat["R1"], mat["R0"], ALU.add)
                    combine(S.WA, mat["W1"], mat["W0"], ALU.add)
                    copy(S.P4, mat["Pd"])
                    copy(S.M4, mat["Md"])
                    combine(S.RB_, mat["R0"], mat["R1"], ALU.add)
                    combine(S.WB, mat["W0"], mat["W1"], ALU.add)
                    copy(S.P8, mat["P2"])
                    copy(S.M8, mat["M2"])
                    combine(S.RC, mat["R1"], mat["R0"], ALU.add)
                    combine(S.WC, mat["W1"], mat["W0"], ALU.add)
                    copy(S.Q_, mat["Q"])
                    copy(S.QT_, mat["QT"])
                    copy(S.Q2T, mat["P2"])
                    combine(S.A_, mat["R0"], mat["R1"], ALU.add)
                    combine(S.Y_, mat["R1"], mat["R0"], ALU.subtract)
                    last(dve.tensor_scalar(Rn, pairs(begin(S.RN), C), -1.0, None, ALU.mult))
                    last(dve.tensor_copy(Us, pairs(begin(S.U_), C)))
                    bs = begin(S.S_)
                    by = begin(S.Y)
                    v(dve.tensor_tensor(Ss, Ss, pairs(bs, C), ALU.add))
                    v(dve.tensor_tensor(Ss, Ss, dec[:, :, c, C:C + 1].to_broadcast([P, CT, C]), ALU.mult))
                    last(dve.tensor_copy(yn, pairs(by, C)))
                    dve.wait_ge(rc_ev, base + S.S_ + 1)
                    mu, vr = st[:, 0:4], st[:, 4:8]
                    v(dve.tensor_reduce(mu, yn, AX_X, ALU.add))
                    v(dve.tensor_scalar(mu, mu, 1.0 / C, None, ALU.mult))
                    v(dve.tensor_tensor(yn, yn, mu.unsqueeze(2).to_broadcast([P, CT, C]), ALU.subtract))
                    v(dve.tensor_tensor(sq, yn, yn, ALU.mult))
                    v(dve.tensor_reduce(vr, sq, AX_X, ALU.add))
                    v(dve.tensor_scalar(vr, vr, 1.0 / C, GN_EPS, ALU.mult, ALU.add))
                    ins = dve.reciprocal(vr, vr)
                    ins.then_inc(rc_var, 1)
                    dve.wait_ge(rc_sd, c + 1)
                    for h in range(2):
                        ins = dve.tensor_tensor(Ybd[H[h], :, h * C:h * C + C], yn[H[h]],
                                                st[H[h], 8:12].unsqueeze(2).to_broadcast([64, CT, C]), ALU.mult)
                    last(ins)
                    b = begin(S.YT)
                    for h in range(2):
                        ins = dve.tensor_copy(yT[H[h], :, c * C:c * C + C], pairs(b)[H[h], :, h * C:h * C + C])
                    last(ins)
                dve.wait_ge(rc_ev, NC * S.COUNT)
                for ct in range(CT):
                    v(dve.tensor_scalar(yT[:, ct, :], yT[:, ct, :], vcol("rwkv_gn_w", ct), vcol("rwkv_gn_b", ct),
                                        ALU.mult, ALU.add))
                v(dve.tensor_tensor(yT, yT, bv, ALU.add))
                v(dve.tensor_tensor(mixT[:, 4:8, :], yT, gate, ALU.mult))
                dve.wait_ge(mod2_mm, 1)
                o, w = SLOTS["mod2"]
                dve.sem_inc(slot_used[(o + w - 1) % RING], 1)
                v(dve.tensor_tensor(mod2[:], psum[7][:, 0:48], vcol("b_mod_2", 0, 48), ALU.add))
                for j, (g, sc) in enumerate((("g_mix_norm_2", 8), ("g_ffn_norm_2", 32))):
                    v(dve.scalar_tensor_tensor(gain[:, 2 + j, :], mod2[:, sc:sc + 8], 1.0, vcol(g, 0, 8),
                                               ALU.add, ALU.mult))

            @block.scalar
            def _(act):
                for c in range(NC):
                    act.wait_ge(rc_var, c + 1)
                    act.activation(st[:, 8:12], st[:, 4:8], ACT.Sqrt).then_inc(rc_sd, 1)
        if STOP == "rwkv":
            return

        def residual_block(tag, name, tiles, rhs, gates, load, width=512, kts=KT, mm_fn=None):
            mm, ev = sem(tag + "_mm"), sem(tag + "_ev")
            with nc.Block() as block:
                @block.sync
                def _(sp):
                    load_slots(sp, *load)

                @block.tensor
                def _(pe):
                    pe_project(pe, name, tiles, rhs, mm, ev, width=width, kts=kts)

                @block.vector
                def _(dve):
                    s0 = SLOTS[name][0]
                    for i, (s, _) in enumerate(tiles):
                        dve.wait_ge(mm, i + 1)
                        dve.scalar_tensor_tensor(xT[:, i, :], psum[i % 8][:, 0:T], gates[:, i:i + 1], xT[:, i, :],
                                                 ALU.mult, ALU.add).then_inc(ev, 1)
                        if i == len(tiles) - 1 or tiles[i + 1][0] != s:
                            dve.sem_inc(slot_used[(s0 + s) % RING], 1)

        eight = [(i // 4, (i % 4) * P) for i in range(8)]
        residual_block("o1", "w_out", eight, mixT, mod1[:, 16:24], (after("mod2"), after("w_out")))
        if STOP == "w_out":
            return
        norm_block("ffn", gain[:, 1, :], mod1[:, 24:32], uT)

        NHP = 2 * HEADS
        qT = area(0, NHP, T)
        utok = area(4096, TT, D)
        wq_mm, wq_ev, ut_mm, ut_ev = sem("wq_mm"), sem("wq_ev"), sem("ut_mm"), sem("ut_ev")
        with nc.Block() as block:
            @block.sync
            def _(sp):
                load_slots(sp, after("w_out"), after("w_q"))

            @block.tensor
            def _(pe):
                for tt in range(TT):
                    for h in range(2):
                        for j in range(4):
                            ins = pe.transpose(psum[4 + 2 * tt + h][:, j * P:(j + 1) * P],
                                               uT[:, 4 * h + j, tt * P:(tt + 1) * P], ident)
                        ins.then_inc(ut_mm, 1)
                pe_project(pe, "w_q", [(i // 4, (i % 4) * P) for i in range(NHP)], uT, wq_mm, wq_ev, banks=4)

            @block.scalar
            def _(act):
                for tt in range(TT):
                    for h in range(2):
                        act.wait_ge(ut_mm, 2 * tt + h + 1)
                        act.copy(utok[:, tt, 512 * h:512 * h + 512], psum[4 + 2 * tt + h][:, :])
                s0 = SLOTS["w_q"][0]
                for i in range(NHP):
                    act.wait_ge(wq_mm, i + 1)
                    if i % 4 == 3:
                        act.sem_inc(slot_used[(s0 + i // 4) % RING], 1)
                    act.copy(qT[:, i, :], psum[i % 4][:, 0:T]).then_inc(wq_ev, 1)

        top = area(6144, TT, NHP, TOPK)
        topi = area(6656, TT, NHP, TOPK)
        topu = area(7168, TT, NHP, TOPK).bitcast(U32)
        work = area(7680, 8, P)
        cand = area(8704, HEADS, TOPK * TOPK)
        cwork = area(10752, HEADS, TOPK * TOPK)
        best = area(12800, TT, HEADS, TOPK)
        posu = area(13056, TT, HEADS, TOPK).bitcast(U32)
        half_u = area(13312, HEADS, TOPK).bitcast(U32)
        half_f = area(13440, HEADS, TOPK)
        pick = area(13568, 2, HEADS, TOPK)
        hot = area(13824, HEADS, TOPK, TOPK)
        prob = area(15872, TT, HEADS, TOPK)
        expert = area(16128, TT, NSEL).bitcast(U32)
        den = area(16384, TT, HEADS)
        best0 = area(16400, TT, HEADS, TOPK)
        sc_mm, tk_ready, tk_best, tk_exp, tk_done = (sem(x) for x in ("sc_mm", "tk_ready", "tk_best", "tk_exp", "tk_done"))
        with nc.Block() as block:
            @block.sync
            def _(sp):
                load_slots(sp, after("w_q"), after("keys"))

            @block.tensor
            def _(pe):
                n = SLOTS["keys"][0]
                wait_slot(pe, n)
                keys = slot(n, NKEYS, NHP)
                for tt in range(TT):
                    for hp in range(NHP):
                        ins = pe.matmul(psum[4 * tt + hp // 4][:, (hp % 4) * P:(hp % 4 + 1) * P],
                                        qT[:, hp, tt * P:(tt + 1) * P], keys[:, hp, :], start=True, stop=True)
                        if hp % 4 == 3:
                            ins.then_inc(sc_mm, 1)

            @block.vector
            def _(dve):
                v = chain("v", dve, seq_v)
                count = [0]

                def lanes(ops, n):
                    for op in ops:
                        for j in range(n):
                            if op is not ops[0]:
                                dve.wait_ge(tk_ready, count[0] - n + 1)
                            op(j).then_inc(tk_ready, 1)
                            count[0] += 1
                    dve.wait_ge(tk_ready, count[0])

                def top16(src, wrk, vals, inds, n):
                    lanes([lambda j: dve.max(vals(j)[:, 0:8], src(j)),
                           lambda j: dve.max_index(inds(j)[:, 0:8], vals(j)[:, 0:8], src(j)),
                           lambda j: dve.match_replace(wrk(j), vals(j)[:, 0:8], src(j), TAKEN),
                           lambda j: dve.max(vals(j)[:, 8:16], wrk(j)),
                           lambda j: dve.max_index(inds(j)[:, 8:16], vals(j)[:, 8:16], wrk(j))], n)

                for tt in range(TT):
                    for g in range(4):
                        dve.wait_ge(sc_mm, 4 * tt + g + 1)
                        if tt == TT - 1 and g == 3:
                            dve.sem_inc(slot_used[SLOTS["keys"][0] % RING], 1)
                        top16(lambda j: psum[4 * tt + g][:, j * P:(j + 1) * P], lambda j: work[:, j, :],
                              lambda j: top[:, tt, 4 * g + j, :], lambda j: topu[:, tt, 4 * g + j, :], 4)
                    v(dve.tensor_copy(topi[:, tt], topu[:, tt]))
                    bc = [P, HEADS, TOPK, TOPK]
                    v(dve.tensor_tensor(cand.rearrange("p h (a b) -> p h a b", a=TOPK),
                                        top[:, tt, 0::2, :].unsqueeze(3).to_broadcast(bc),
                                        top[:, tt, 1::2, :].unsqueeze(2).to_broadcast(bc), ALU.add))
                    top16(lambda j: cand[:, j, :], lambda j: cwork[:, j, :], lambda j: best[:, tt, j, :],
                          lambda j: posu[:, tt, j, :], HEADS)
                    dve.tensor_tensor(best0[:, tt], best[:, tt], best[:, tt, :, 0:1].to_broadcast([P, HEADS, TOPK]),
                                      ALU.subtract).then_inc(tk_best, 1)
                    for half, (op, by) in enumerate(((ALU.logical_shift_right, 4), (ALU.bitwise_and, 15))):
                        v(dve.tensor_scalar(half_u, posu[:, tt], by, None, op))
                        v(dve.tensor_copy(half_f, half_u))
                        v(dve.tensor_tensor(hot, half_f.unsqueeze(3).to_broadcast(bc),
                                            cst("iota").unsqueeze(1).unsqueeze(1).to_broadcast(bc), ALU.is_equal))
                        v(dve.tensor_tensor(hot, hot, topi[:, tt, half::2, :].unsqueeze(2).to_broadcast(bc), ALU.mult))
                        v(dve.tensor_reduce(pick[:, half], hot, AX_X, ALU.add))
                    v(dve.scalar_tensor_tensor(pick[:, 0], pick[:, 0], float(NKEYS), pick[:, 1], ALU.mult, ALU.add))
                    v(dve.tensor_copy(expert[:, tt].rearrange("p (h k) -> p h k", h=HEADS), pick[:, 0]))
                    dve.wait_ge(tk_exp, tt + 1)
                    v(dve.tensor_reduce(den[:, tt], prob[:, tt], AX_X, ALU.add))
                    v(dve.reciprocal(den[:, tt], den[:, tt]))
                    v(dve.tensor_tensor(prob[:, tt], prob[:, tt], den[:, tt].unsqueeze(2).to_broadcast([P, HEADS, TOPK]),
                                        ALU.mult))

            @block.scalar
            def _(act):
                for tt in range(TT):
                    act.wait_ge(tk_best, tt + 1)
                    act.activation(prob[:, tt], best0[:, tt], ACT.Exp).then_inc(tk_exp, 1)
        if STOP == "topk":
            return

        HALF = GRING
        BODY = 2 * HALF
        DIAGS = 4
        rows = area(10752, GRING, 2 * D)
        ROWS_AT = 10752
        prob2 = area(0, TT, NSEL)
        expert2 = area(256, TT, NSEL).bitcast(U32)
        stage = area(512, 2, HALF).bitcast(U32)
        pstage = area(528, BODY)
        hdot = area(544, BODY)
        hgel = area(560, BODY)
        zrow = area(576, 512)
        diag = area(1088, DIAGS, P)
        dump = area(1600, D)
        ptok = area(6144, TT, D)
        assert ROWS_AT + GRING * 2 * D <= ARENA and ROWS_AT >= 6144 + TT * D
        pe_copied = sem("pe_copied")
        row_loaded = [sem(f"row_loaded{j}") for j in range(GRING)]
        staged, pstaged, rows_used, dotted, gelued, diag_ready, z_ready, turn = (
            sem(x) for x in ("staged", "pstaged", "rows_used", "dotted", "gelued", "diag_ready", "z_ready", "turn"))
        px_ev, px_mm = sem("px_ev"), sem("px_mm")
        with nc.Block() as block:
            @block.vector
            def _(dve):
                dve.tensor_copy(prob2, prob.rearrange("p t h k -> p t (h k)"))
                dve.tensor_copy(expert2, expert)
        LOOPS = NSEL // BODY
        with nc.Block() as block:
            @block.gpsimd
            def _(pool):
                for tt in range(TT):
                    with pool.Fori(0, LOOPS) as i:
                        for half in range(2):
                            k = 2 * (tt * LOOPS) + half
                            pool.wait_ge(rows_used, i * BODY + (tt * NSEL + half * HALF + 1))
                            pool.tensor_copy(stage[:, half, :], expert2[:, tt, bass.ds(i * BODY + half * HALF, HALF)]
                                             ).then_inc(staged, 1)
                            pool.wait_ge(staged, i * 2 + (k + 1))
                            pool.sem_inc(turn, 1)
                            for j in range(HALF):
                                pool.wait_ge(rows_used, i * BODY + (tt * NSEL + half * HALF + j + 1))
                                pool.sem_inc(turn, 1)
                                pool.indirect_dma_start(rows[:, j, :], None, experts_in,
                                                        bass.IndirectOffsetOnAxis(ap=stage[:, half, j:j + 1], axis=0)
                                                        ).then_inc(row_loaded[j], 16)

            @block.vector
            def _(dve):
                v = chain("v", dve, seq_v)
                dve.memset(zrow, 0.0).then_inc(z_ready, 1)
                dve.sem_inc(diag_ready, 1)

                def make_diag(tt, i, q):
                    dve.wait_ge(gelued, i * BODY + (tt * NSEL + q + 1))
                    dve.wait_ge(rows_used, i * BODY + (tt * NSEL + q + GRING - DIAGS + 1))
                    dve.tensor_scalar(diag[:, q % DIAGS, :], ident, hgel[:, q:q + 1], pstage[:, q:q + 1],
                                      ALU.mult, ALU.mult).then_inc(diag_ready, 1)

                for tt in range(TT):
                    with dve.Fori(0, LOOPS) as i:
                        dve.wait_ge(diag_ready, i * BODY + (tt * NSEL + 1))
                        dve.tensor_copy(pstage, prob2[:, tt, bass.ds(i * BODY, BODY)]).then_inc(pstaged, 1)
                        dve.wait_ge(pstaged, i + (tt * LOOPS + 1))
                        for q in range(BODY):
                            dve.wait_ge(row_loaded[q % GRING], i * 32 + (tt * LOOPS * 32 + 16 * (q // GRING + 1)))
                            dve.tensor_tensor_reduce(dump, rows[:, q % GRING, 0:D], utok[:, tt, :], 1.0, 0.0,
                                                     ALU.mult, ALU.add, hdot[:, q:q + 1]).then_inc(dotted, 1)
                            if q:
                                make_diag(tt, i, q - 1)
                            dve.wait_ge(dotted, i * BODY + (tt * NSEL + q + 1))
                        make_diag(tt, i, BODY - 1)

            @block.scalar
            def _(act):
                for tt in range(TT):
                    with act.Fori(0, LOOPS) as i:
                        for q in range(BODY):
                            act.wait_ge(dotted, i * BODY + (tt * NSEL + q + 1))
                            act.activation(hgel[:, q:q + 1], hdot[:, q:q + 1], ACT.Gelu).then_inc(gelued, 1)

            @block.tensor
            def _(pe):
                pe.wait_ge(z_ready, 1)
                for b in range(2 * TT):
                    pe.matmul(psum[b][:, :], ident, zrow, start=True, stop=False, skip_group_check=True)
                pe.sem_inc(rows_used, GRING)
                for tt in range(TT):
                    with pe.Fori(0, LOOPS) as i:
                        for q in range(BODY):
                            pe.wait_ge(diag_ready, i * BODY + (tt * NSEL + q + 2))
                            for h in range(2):
                                ins = pe.matmul(psum[2 * tt + h][:, :], diag[:, q % DIAGS, :],
                                                rows[:, q % GRING, D + 512 * h:D + 512 * h + 512],
                                                start=False, stop=False, skip_group_check=True)
                            ins.then_inc(rows_used, 1)
        with nc.Block() as block:
            @block.scalar
            def _(act):
                for tt in range(TT):
                    for h in range(2):
                        act.copy(ptok[:, tt, 512 * h:512 * h + 512], psum[2 * tt + h][:, :]).then_inc(px_ev, 1)

            @block.tensor
            def _(pe):
                pe.wait_ge(px_ev, 2 * TT)
                for b in range(4):
                    for kk in range(2):
                        for tt in range(TT):
                            k = 2 * b + kk
                            ins = pe.transpose(psum[4 + b][:, kk * T + tt * P:kk * T + (tt + 1) * P],
                                               ptok[:, tt, k * P:(k + 1) * P], ident)
                    ins.then_inc(px_mm, 1)

            @block.vector
            def _(dve):
                for k in range(KT):
                    dve.wait_ge(px_mm, k // 2 + 1)
                    dve.scalar_tensor_tensor(xT[:, k, :], psum[4 + k // 2][:, (k % 2) * T:(k % 2 + 1) * T],
                                             mod1[:, 40 + k:41 + k], xT[:, k, :], ALU.mult, ALU.add)
        if STOP == "peer":
            return

        norm_block("fin", vcol("final_g", 0, 8), None, uT)
        with nc.Block() as block:
            @block.scalar
            def _(act):
                act.copy(xT[:, :, :], uT[:, :, :])
        norm_block("mix2", gain[:, 2, :], mod2[:, 0:8], uT)

        qk = area(0, 16, T)
        qki = area(4096, 5, T)
        vtok = area(5376, 2, TT, CH)
        sgate = area(7424, 2 * KT, T)
        wi = area(11520, TT, HEADS)
        IDX_SCALE = (8 ** -0.5) * (64 ** -0.5)
        full = slice(0, P)

        def item(kind, s, col, dst, func=ACT.Copy, scale=1.0):
            return kind, s, col, dst, func, scale
        items = [item("feat", 0, i * P, qk[:, i, :]) for i in range(4)]
        items += [item("feat", 1, i * P, qk[:, 4 + i, :]) for i in range(4)]
        items += [item("token", 2, tt, vtok[:, 0, tt, :]) for tt in range(TT)]
        items += [item("feat", 3, i * P, qki[:, i, :]) for i in range(4)]
        items += [item("key", 4, 0, qki[:, 4, :])]
        items += [item("weight", 4, tt, wi[:, tt, :], scale=IDX_SCALE) for tt in range(TT)]
        items += [item("feat", 5, i * P, qk[:, 8 + i, :]) for i in range(4)]
        items += [item("feat", 6, i * P, qk[:, 12 + i, :]) for i in range(4)]
        items += [item("token", 7, tt, vtok[:, 1, tt, :]) for tt in range(TT)]
        items += [item("feat", 8 + i // 4, (i % 4) * P, sgate[:, i, :], ACT.Sigmoid) for i in range(16)]
        i2_mm, i2_ev = sem("i2_mm"), sem("i2_ev")
        with nc.Block() as block:
            @block.sync
            def _(sp):
                load_slots(sp, after("keys"), after("w_in2"))

            @block.tensor
            def _(pe):
                s0 = SLOTS["w_in2"][0]
                for n, (kind, s, col, *_) in enumerate(items):
                    if n == 0 or items[n - 1][1] != s:
                        wait_slot(pe, s0 + s)
                    if n >= 8:
                        pe.wait_ge(i2_ev, n - 7)
                    bank, w = psum[n % 8], slot(s0 + s)
                    for half in range(2 if kind == "key" else 1):
                        for k in range(KT):
                            if kind == "feat":
                                o, l, r = bank[:, 0:T], w[:, k, col:col + P], uT[:, k, :]
                            elif kind == "key":
                                o, l, r = bank[64 * half:64 * half + 64, 0:T], w[:, k, 0:64], uT[:, k, :]
                            elif kind == "token":
                                o, l, r = bank[:, :], uT[:, k, col * P:(col + 1) * P], w[:, k, :]
                            else:
                                o, l, r = bank[:, 0:HEADS], uT[:, k, col * P:(col + 1) * P], w[:, k, 64:64 + HEADS]
                            ins = pe.matmul(o, l, r, start=(k == 0), stop=(k == KT - 1))
                    ins.then_inc(i2_mm, 1)

            @block.scalar
            def _(act):
                s0 = SLOTS["w_in2"][0]
                for n, (kind, s, col, dst, func, scale) in enumerate(items):
                    act.wait_ge(i2_mm, n + 1)
                    if n == len(items) - 1 or items[n + 1][1] != s:
                        act.sem_inc(slot_used[(s0 + s) % RING], 1)
                    width = {"feat": T, "key": T, "token": CH, "weight": HEADS}[kind]
                    act.activation(dst, psum[n % 8][:, 0:width], func, scale=scale).then_inc(i2_ev, 1)
        if STOP == "w_in2":
            return

        rope = slot(SLOTS["rope"][0], P, 32).rearrange("p k n -> p (k n)")
        cos, sin = (rope[:, 0:T], rope[:, 512:512 + T]), (rope[:, T:512], rope[:, 512 + T:1024])
        causal = rope[:, 1024:1536].rearrange("p (t s) -> p t s", t=TT)
        rot = (rope[:, 1536:1664], rope[:, 1664:1792])
        rs = area(11552, 16, T)
        ro = area(15648, 4, 2, T)
        GROUPS = 19
        hr = {x: sem("hr_" + x) for x in ("sq", "mm", "iev", "sev", "rec", "nrm", "cs", "rev", "fin")}
        gains2 = ("g_q_dsa_2", "g_k_dsa_2", "g_q_moba_2", "g_k_moba_2")
        with nc.Block() as block:
            @block.tensor
            def _(pe):
                wait_slot(pe, SLOTS["rope"][0])
                for g in range(GROUPS):
                    bank = psum[g % 8]
                    if 8 <= g < 11:
                        pe.wait_ge(hr["iev"], g - 7)
                    if g >= 11:
                        pe.wait_ge(hr["sev"], g - 10)
                        pe.wait_ge(hr["nrm"], 2 * (g - 11) + 2)
                    if 3 <= g < 11:
                        pe.wait_ge(hr["sq"], (g - 3) // 2 + 1)
                    for j in range(2):
                        if g < 3:
                            if 2 * g + j == 5:
                                continue
                            l, r = rot[1], qki[:, 2 * g + j, :]
                        elif g < 11:
                            l, r = ones, rs[:, 2 * (g - 3) + j, :]
                        else:
                            l, r = rot[0], qk[:, 2 * (g - 11) + j, :]
                        ins = pe.matmul(bank[:, j * T:(j + 1) * T], l, r, start=True, stop=True)
                    ins.then_inc(hr["mm"], 1)

            @block.scalar
            def _(act):
                for i in range(4):
                    act.activation(rs[:, 4 * i:4 * i + 4, :], qk[:, 4 * i:4 * i + 4, :], ACT.Square).then_inc(hr["sq"], 1)
                for g in range(3, 11):
                    act.wait_ge(hr["mm"], g + 1)
                    act.activation(rs[:, 2 * g - 6:2 * g - 4, :], psum[g % 8][:, :].rearrange("p (j t) -> p j t", j=2),
                                   ACT.Sqrt, bias=epsc[:, 0:1], scale=1.0 / HD).then_inc(hr["sev"], 1)

            @block.vector
            def _(dve):
                wait_slot(dve, SLOTS["rope"][0])
                v = chain("v", dve, seq_v)

                def rotate(g, x, n, which, base):
                    dve.wait_ge(hr["mm"], g + 1)
                    t = ro[:, g % 4, 0:n, :]
                    s = [P, n, T]
                    ps = psum[g % 8][:, 0:n * T].rearrange("p (j t) -> p j t", j=n)
                    v(dve.tensor_tensor(t, ps, sin[which].unsqueeze(1).to_broadcast(s), ALU.mult))
                    dve.sem_inc(hr[base], 1)
                    v(dve.tensor_tensor(x, x, cos[which].unsqueeze(1).to_broadcast(s), ALU.mult))
                    dve.tensor_tensor(x, x, t, ALU.add).then_inc(hr["fin"], 1)

                for g in range(3):
                    n = 1 if g == 2 else 2
                    rotate(g, qki[:, 2 * g:2 * g + n, :], n, 1, "iev")
                for i in range(8):
                    dve.wait_ge(hr["sev"], i + 1)
                    v(dve.reciprocal(rs[:, 2 * i:2 * i + 2, :], rs[:, 2 * i:2 * i + 2, :]))
                    for j in (2 * i, 2 * i + 1):
                        dve.scalar_tensor_tensor(qk[:, j, :], qk[:, j, :], vcol(gains2[j // 4]), rs[:, j, :],
                                                 ALU.mult, ALU.mult).then_inc(hr["nrm"], 1)
                for i in range(8):
                    rotate(11 + i, qk[:, 2 * i:2 * i + 2, :], 2, 0, "rev")
        if STOP == "rope":
            return

        relu = area(0 + 15648, 4, T)
        score = area(16672, TT, T)
        left = area(17184, TT, T)
        max8 = area(17696, TT, 8)
        maskd = area(17712, TT, T)
        ix_mm, ix_relu, ix_acc, ix_top = sem("ix_mm"), sem("ix_relu"), sem("ix_acc"), sem("ix_top")
        width = [P * (tt + 1) for tt in range(TT)]
        with nc.Block() as block:
            @block.tensor
            def _(pe):
                for n in range(TT * HEADS):
                    tt, h = n // HEADS, n % HEADS
                    s = slice(64 * (h % 2), 64 * (h % 2) + 64)
                    if n >= 8:
                        pe.wait_ge(ix_relu, n - 7)
                    pe.matmul(psum[n % 8][:, 0:width[tt]], qki[s, h // 2, tt * P:(tt + 1) * P],
                              qki[s, 4, 0:width[tt]], start=True, stop=True).then_inc(ix_mm, 1)

            @block.scalar
            def _(act):
                for n in range(TT * HEADS):
                    tt = n // HEADS
                    act.wait_ge(ix_mm, n + 1)
                    if n >= 4:
                        act.wait_ge(ix_acc, n - 3)
                    act.activation(relu[:, n % 4, 0:width[tt]], psum[n % 8][:, 0:width[tt]],
                                   ACT.Relu).then_inc(ix_relu, 1)

            @block.vector
            def _(dve):
                for n in range(TT * HEADS):
                    tt, h = n // HEADS, n % HEADS
                    dve.wait_ge(ix_relu, n + 1)
                    if h:
                        dve.wait_ge(ix_acc, n)
                    dst = score[:, tt, 0:width[tt]]
                    prev = causal[:, tt, 0:width[tt]] if h == 0 else dst
                    dve.scalar_tensor_tensor(dst, relu[:, n % 4, 0:width[tt]], wi[:, tt, h:h + 1], prev,
                                             ALU.mult, ALU.add).then_inc(ix_acc, 1)
                dve.wait_ge(ix_acc, TT * HEADS)
                count = 0
                for r in range(DSA_TOPK // 8):
                    for op in range(2):
                        for tt in range(TT):
                            src = score if r == 0 else left
                            if r or op:
                                dve.wait_ge(ix_top, count - TT + 1)
                            if op == 0:
                                ins = dve.max(max8[:, tt, :], src[:, tt, 0:width[tt]])
                            else:
                                ins = dve.match_replace(left[:, tt, 0:width[tt]], max8[:, tt, :],
                                                        src[:, tt, 0:width[tt]], TAKEN)
                            ins.then_inc(ix_top, 1)
                            count += 1
                v = chain("v", dve, seq_v)
                dve.wait_ge(ix_top, count)
                for tt in range(TT):
                    w = slice(0, width[tt])
                    v(dve.tensor_scalar(maskd[:, tt, w], left[:, tt, w], TAKEN / 2, NEG, ALU.is_gt, ALU.mult))
                    v(dve.tensor_tensor(maskd[:, tt, w], maskd[:, tt, w], causal[:, tt, w], ALU.add))
        if STOP == "idx":
            return

        NI = 16
        sm = area(18224, 4, T)
        pT = area(19248, 2, T)
        nmax, psm, rsm = area(19760, NI), area(19776, NI), area(19792, NI)
        at = {x: sem("at_" + x) for x in ("s", "sm", "max", "exp", "rec", "p", "t", "pT", "o", "oT")}

        def what(n):
            b, h, tt = n // 8, n // 2 % 4, n % 2
            return b, h, tt, width[tt]
        with nc.Block() as block:
            @block.sync
            def _(sp):
                load_slots(sp, after("w_in2"), after("rope"))

            @block.tensor
            def _(pe):
                def scores(n):
                    b, h, tt, w = what(n)
                    if n >= 4:
                        pe.wait_ge(at["sm"], n - 3)
                    pe.matmul(psum[n % 4][:, 0:w], qk[:, 8 * b + h, tt * P:(tt + 1) * P], qk[:, 8 * b + 4 + h, 0:w],
                              start=True, stop=True).then_inc(at["s"], 1)

                def flips(n):
                    b, h, tt, w = what(n)
                    pe.wait_ge(at["p"], n + 1)
                    if n >= 2:
                        pe.wait_ge(at["pT"], n - 1)
                    for st_ in range(tt + 1):
                        ins = pe.transpose(psum[4 + n % 2][:, st_ * P:(st_ + 1) * P],
                                           sm[:, n % 4, st_ * P:(st_ + 1) * P], ident)
                    ins.then_inc(at["t"], 1)

                def values(n):
                    b, h, tt, w = what(n)
                    pe.wait_ge(at["pT"], n + 1)
                    if n >= 2:
                        pe.wait_ge(at["oT"], n - 1)
                    for st_ in range(tt + 1):
                        ins = pe.matmul(psum[6 + n % 2][:, 0:P], vtok[:, b, st_, h * HD:(h + 1) * HD],
                                        pT[:, n % 2, st_ * P:(st_ + 1) * P], start=(st_ == 0), stop=(st_ == tt))
                    ins.then_inc(at["o"], 1)
                for n in range(NI + 3):
                    if n < NI:
                        scores(n)
                    if 2 <= n < NI + 2:
                        flips(n - 2)
                    if n >= 3:
                        values(n - 3)

            @block.vector
            def _(dve):
                for n in range(NI + 1):
                    if n < NI:
                        b, h, tt, w = what(n)
                        dve.wait_ge(at["s"], n + 1)
                        if n >= 4:
                            dve.wait_ge(at["t"], n - 3)
                        mask = (causal if b else maskd)[:, tt, 0:w]
                        dve.scalar_tensor_tensor(sm[:, n % 4, 0:w], psum[n % 4][:, 0:w], HD ** -0.5, mask,
                                                 ALU.mult, ALU.add).then_inc(at["sm"], 1)
                        dve.wait_ge(at["sm"], n + 1)
                        dve.tensor_reduce(nmax[:, n:n + 1], sm[:, n % 4, 0:w], AX_X, ALU.max,
                                          negate=True).then_inc(at["max"], 1)
                    if n:
                        m, w = n - 1, what(n - 1)[3]
                        dve.wait_ge(at["exp"], m + 1)
                        dve.reciprocal(rsm[:, m:m + 1], psm[:, m:m + 1]).then_inc(at["rec"], 1)
                        dve.wait_ge(at["rec"], m + 1)
                        dve.tensor_scalar(sm[:, m % 4, 0:w], sm[:, m % 4, 0:w], rsm[:, m:m + 1], None,
                                          ALU.mult).then_inc(at["p"], 1)
                dve.sem_inc(slot_used[SLOTS["rope"][0] % RING], 1)

            @block.scalar
            def _(act):
                for n in range(NI + 3):
                    if n < NI:
                        b, h, tt, w = what(n)
                        act.wait_ge(at["max"], n + 1)
                        act.activation(sm[:, n % 4, 0:w], sm[:, n % 4, 0:w], ACT.Exp, bias=nmax[:, n:n + 1],
                                       accum_out=psm[:, n:n + 1]).then_inc(at["exp"], 1)
                    if 2 <= n < NI + 2:
                        m, w = n - 2, what(n - 2)[3]
                        act.wait_ge(at["t"], m + 1)
                        if m >= 2:
                            act.wait_ge(at["o"], m - 1)
                        act.copy(pT[:, m % 2, 0:w], psum[4 + m % 2][:, 0:w]).then_inc(at["pT"], 1)
                    if n >= 3:
                        b, h, tt, w = what(n - 3)
                        act.wait_ge(at["o"], n - 2)
                        act.copy(mixT[:, 4 * b + h, tt * P:(tt + 1) * P], psum[6 + (n - 3) % 2][:, 0:P]).then_inc(at["oT"], 1)
        if STOP == "attn":
            return

        merged = area(15648, KT, T)
        gated = area(17696, 4, T)
        br_mm, br_ev, br_t = sem("br_mm"), sem("br_ev"), sem("br_t")
        with nc.Block() as block:
            @block.sync
            def _(sp):
                load_slots(sp, after("rope"), after("w_br"))

            @block.tensor
            def _(pe):
                s0 = SLOTS["w_br"][0]
                for n in range(16):
                    b, m = n // 8, n % 8
                    if m == 0:
                        wait_slot(pe, s0 + b)
                    if n >= 8:
                        pe.wait_ge(br_ev, n - 7)
                    for k in range(4):
                        ins = pe.matmul(psum[n % 8][:, 0:T], slot(s0 + b, D, 4)[:, k, m * P:(m + 1) * P],
                                        mixT[:, 4 * b + k, :], start=(k == 0), stop=(k == 3))
                    ins.then_inc(br_mm, 1)

            @block.vector
            def _(dve):
                s0 = SLOTS["w_br"][0]
                for n in range(16):
                    b, m = n // 8, n % 8
                    dve.wait_ge(br_mm, n + 1)
                    if m == 7:
                        dve.sem_inc(slot_used[(s0 + b) % RING], 1)
                    dst = gated[:, m % 4, :] if b else merged[:, m, :]
                    if b and m >= 4:
                        dve.wait_ge(br_t, m - 3)
                    dve.tensor_tensor(dst, psum[n % 8][:, 0:T], sgate[:, n, :], ALU.mult).then_inc(br_ev, 1)
                    if b:
                        dve.wait_ge(br_ev, n + 1)
                        dve.tensor_tensor(merged[:, m, :], merged[:, m, :], dst, ALU.add).then_inc(br_t, 1)
        if STOP == "merged":
            return
        residual_block("o2", "w_out2", eight, merged, mod2[:, 16:24], (after("w_br"), after("w_out2")))
        norm_block("ffn2", gain[:, 3, :], mod2[:, 24:32], uT)
        ff = area(0, FT, T)
        gu_mm, gu_act, gu_ev = sem("gu_mm"), sem("gu_act"), sem("gu_ev")
        NGU = SLOTS["w_gu"][1]
        with nc.Block() as block:
            @block.sync
            def _(sp):
                load_slots(sp, after("w_out2"), after("w_gu"))

            @block.tensor
            def _(pe):
                s0 = SLOTS["w_gu"][0]
                for n in range(4 * NGU):
                    s, j = n // 4, n % 4
                    if j == 0:
                        wait_slot(pe, s0 + s)
                    if s >= 2:
                        if j < 2:
                            pe.wait_ge(gu_act, 2 * (s - 2) + j + 1)
                        else:
                            pe.wait_ge(gu_ev, 2 * (s - 2) + j - 1)
                    for k in range(KT):
                        ins = pe.matmul(psum[n % 8][:, 0:T], slot(s0 + s)[:, k, j * P:(j + 1) * P], uT[:, k, :],
                                        start=(k == 0), stop=(k == KT - 1))
                    ins.then_inc(gu_mm, 1)

            @block.scalar
            def _(act):
                for n in range(2 * NGU):
                    s, j = n // 2, n % 2
                    act.wait_ge(gu_mm, 4 * s + j + 1)
                    act.activation(ff[:, n, :], psum[(4 * s + j) % 8][:, 0:T], ACT.Silu).then_inc(gu_act, 1)

            @block.vector
            def _(dve):
                for n in range(2 * NGU):
                    s, j = n // 2, n % 2
                    dve.wait_ge(gu_mm, 4 * s + j + 3)
                    dve.wait_ge(gu_act, n + 1)
                    dve.tensor_tensor(ff[:, n, :], ff[:, n, :], psum[(4 * s + 2 + j) % 8][:, 0:T],
                                      ALU.mult).then_inc(gu_ev, 1)
                    if j == 1:
                        dve.sem_inc(slot_used[(SLOTS["w_gu"][0] + s) % RING], 1)
        residual_block("dn", "w_down", [(i, 0) for i in range(8)], ff, mod2[:, 40:48],
                       (after("w_gu"), NSLOTS), width=P, kts=FT)
        out_done = sem("out_done")
        with nc.Block() as block:
            @block.sync
            def _(sp):
                sp.dma_start(out, xT[:]).then_inc(out_done, 16)
                sp.wait_ge(out_done, 16)

STOP = None


def kernel(**inputs):
    import concourse.bacc as bacc
    from concourse.bass_utils import run_bass_kernel_spmd

    w = {k: np.asarray(v) for k, v in inputs.items()}

    def cols(a):
        return np.asarray(a).reshape(-1, P).T

    vecs = np.ascontiguousarray(np.concatenate([cols(w[name]) for name, _ in VECS], axis=1))

    slots = np.zeros((NSLOTS, P, SLOT), np.float32)

    def tiles(n, a):
        k = a.shape[0] // P
        slots[n, :, 0:k * a.shape[1]] = a.reshape(k, P, -1).transpose(1, 0, 2).reshape(P, -1)

    def fill(name, a, width=512):
        s0, n = SLOTS[name]
        for s in range(n):
            tiles(s0 + s, a[:, s * width:(s + 1) * width])

    fill("ada", w["ada_w"][0])
    fill("w_in", w["w_in"][0][:, :2560])
    wi = w["w_in"][0][:, 2560:]
    tiles(SLOTS["w_in"][0] + 5, np.concatenate([wi, np.zeros((D, 256), np.float32)], axis=1))
    s = SLOTS["lora"][0]
    slots[s, 0:64, 0:CH] = w["rwkv_w2"][0]
    slots[s, 64:128, 0:CH] = w["rwkv_a2"][0]
    slots[s, :, CH:2 * CH] = w["rwkv_g2"][0]
    fill("mod2", w["w_mod_2"][0])
    fill("w_out", w["w_out"][0])
    fill("w_q", w["peer_w_q"][0])
    slots[SLOTS["keys"][0], :, 0:2048] = w["peer_sub_keys"][0].reshape(16, NKEYS, P).transpose(2, 0, 1).reshape(P, -1)
    wi = w["w_in_2"][0]
    s = SLOTS["w_in2"][0]
    for j in range(4):
        tiles(s + j, wi[:, j * 512:(j + 1) * 512])
    tiles(s + 4, np.concatenate([wi[:, 2048:2120], np.zeros((D, 440), np.float32)], axis=1))
    for j in range(7):
        tiles(s + 5 + j, wi[:, 2120 + j * 512:2120 + (j + 1) * 512])
    consts, rope = shape_constants()
    slots[SLOTS["rope"][0]] = rope
    tiles(SLOTS["w_br"][0], w["w_br_dsa_2"][0])
    tiles(SLOTS["w_br"][0] + 1, w["w_br_moba_2"][0])
    fill("w_out2", w["w_out_2"][0])
    gu = w["w_gate_up_2"][0]
    for j in range(11):
        tiles(SLOTS["w_gu"][0] + j, np.concatenate([gu[:, j * 256:(j + 1) * 256],
                                                    gu[:, FF + j * 256:FF + (j + 1) * 256]], axis=1))
    fill("w_down", w["w_down_2"][0], P)
    experts = np.concatenate([w["peer_u"][0], w["peer_v"][0]], axis=1)
    xT = np.ascontiguousarray(w["x"][0].T.reshape(KT, P, T).transpose(1, 0, 2))

    nc = bacc.Bacc("TRN2", target_bir_lowering=False, num_devices=1)
    arrays = {"xT_in": xT, "vecs_in": vecs, "consts_in": consts, "slots_in": slots, "experts_in": experts}
    args = [nc.dram_tensor(k, a.shape, mybir.dt.from_np(a.dtype), kind="ExternalInput").ap()
            for k, a in arrays.items()]
    out = nc.dram_tensor("out_dram", (P, KT, T), F32, kind="ExternalOutput").ap()
    build(nc, *args, out)
    r = run_bass_kernel_spmd(nc, [arrays], core_ids=[0])
    o = r.results[0]["out_dram"]
    return np.ascontiguousarray(o.transpose(1, 0, 2).reshape(D, T).T).reshape(1, T, D)
```

```python
from contextlib import ExitStack

import numpy as np
import concourse.bass as bass
from concourse import mybir

ALU = mybir.AluOpType
ACT = mybir.ActivationFunctionType
F32 = mybir.dt.float32
U32 = mybir.dt.uint32
AX_X = mybir.AxisListType.X

P = 128
D = 1024
KT = D // P
T = 256
TT = T // P
CH = 512
CT = CH // P
TAPS = 31
NPROJ = 14
C = 64
NC = T // C
HEADS, NKEYS, TOPK = 8, 128, 16
NSEL = HEADS * TOPK
DSA_TOPK = 64
FF = 2816
FT = FF // P
HD = 128
NEG = -1e30
TAKEN = -3e38
RMS_EPS, LN_EPS, GN_EPS = 1e-6, 1e-5, 64e-5
RING = 4
SLOT = KT * 512
GRING = 8

VECS = [("ada_b", 48), ("norm_mix_g", 8), ("conv_dw_w", TAPS * CT), ("conv_dw_b", CT), ("conv_ln_w", CT),
        ("conv_ln_b", CT), ("rwkv_mu", NPROJ), ("rwkv_w0", CT), ("rwkv_a0", CT), ("rwkv_k_k", CT),
        ("rwkv_k_a", CT), ("rwkv_r_k", CT), ("rwkv_gn_w", CT), ("rwkv_gn_b", CT), ("norm_ffn_g", 8),
        ("final_g", 8), ("c", 8), ("c_2", 8), ("b_mod_2", 48), ("g_mix_norm_2", 8), ("g_ffn_norm_2", 8),
        ("g_q_dsa_2", 1), ("g_k_dsa_2", 1), ("g_q_moba_2", 1), ("g_k_moba_2", 1)]
VCOL, _n = {}, 0
for _name, _w in VECS:
    VCOL[_name] = _n
    _n += _w
NVEC = _n

CONSTS = [("ident", P), ("ones", P), ("bones", P), ("dS", C), ("oS", C), ("mS", C), ("mI", C), ("dL", C),
          ("oL", C), ("eye", C), ("chunk", T), ("iota", TOPK)]
CCOL, _n = {}, 0
for _name, _w in CONSTS:
    CCOL[_name] = (_n, _w)
    _n += _w
NCONST = _n

SLOTS = {}
_n = 0
for _name, _w in [("ada", 4), ("w_in", 6), ("ada2", 2), ("lora", 1), ("ada3", 6), ("w_out", 2), ("w_q", 4),
                  ("keys", 1), ("mod2", 12),
                  ("w_in2", 12), ("rope", 1), ("w_br", 2), ("w_out2", 2), ("w_gu", 11), ("w_down", 8)]:
    SLOTS[_name] = (_n, _w)
    _n += _w
NSLOTS = _n


def shape_constants():
    c = np.zeros((P, NCONST), np.float32)

    def put(name, a):
        o, w = CCOL[name]
        c[:, o:o + w] = a
    r = np.arange(P)[:, None] % C
    q = np.arange(C)[None, :]
    same = r // 16 == q // 16
    put("ident", np.eye(P))
    put("ones", 1.0)
    put("bones", np.arange(P)[:, None] // C == np.arange(P)[None, :] // C)
    put("dS", (r < q) & same)
    put("oS", (r < q) & ~same)
    put("mS", r < q)
    put("mI", r <= q)
    put("dL", (q < r) & same)
    put("oL", (q < r) & ~same)
    put("eye", r == q)
    put("chunk", np.arange(T)[None, :] % C != 0)
    put("iota", np.arange(TOPK)[None, :])

    rope = np.zeros((P, SLOT), np.float32)
    for n, dim in enumerate((HD, 64)):
        inv = 10000.0 ** (-np.arange(0, dim, 2, dtype=np.float32) / np.float32(dim))
        ang = (np.arange(T, dtype=np.float32)[:, None] * inv[None, :].astype(np.float32)).T
        reps = P // (dim // 2)
        rope[:, n * 512:n * 512 + T] = np.tile(np.cos(ang), (reps, 1))
        rope[:, n * 512 + T:n * 512 + 512] = np.tile(np.sin(ang), (reps, 1))
        rot = np.zeros((P, P), np.float32)
        for i in range(P):
            if i % dim < dim // 2:
                rot[i + dim // 2, i] = -1.0
            else:
                rot[i - dim // 2, i] = 1.0
        rope[:, 1536 + n * P:1536 + (n + 1) * P] = rot
    t = np.arange(TT)[None, :, None] * P + np.arange(P)[:, None, None]
    rope[:, 1024:1536] = np.where(np.arange(T)[None, None, :] <= t, 0.0, NEG).reshape(P, 512)
    return c, rope


def build(nc, xT_in, vecs_in, consts_in, slots_in, experts_in, out):
    with ExitStack() as ctx:
        def sb(name, shape, dt=F32):
            return ctx.enter_context(nc.sbuf_tensor(name, shape, dt))

        def sem(name):
            return ctx.enter_context(nc.semaphore(name))

        psum = [ctx.enter_context(nc.psum_tensor(f"bank{i}", [P, 512], F32)) for i in range(8)]
        ring = sb("ring", [P, RING, SLOT])
        xT = sb("xT", [P, KT, T])
        uT = sb("uT", [P, KT, T])
        mixT = sb("mixT", [P, KT, T])
        vec = sb("vec", [P, NVEC])
        con = sb("con", [P, NCONST])
        mod1 = sb("mod1", [P, 48])
        mod2 = sb("mod2", [P, 48])
        gain = sb("gain", [P, 4, KT])
        csil = sb("csil", [P, 2, KT])
        rstd = sb("rstd", [P, T])
        epsc = sb("epsc", [P, 4])
        ARENA = 28500
        arena = sb("arena", [P, ARENA])

        def area(at, *shape):
            n = int(np.prod(shape))
            assert at + n <= ARENA, (at, shape)
            a = arena[:, at:at + n]
            if len(shape) == 1:
                return a
            names = "abcde"[:len(shape)]
            kw = {k: s for k, s in zip(names[1:], shape[1:])}
            return a.rearrange(f"p ({' '.join(names)}) -> p {' '.join(names)}", **kw)

        def cst(name):
            o, w = CCOL[name]
            return con[:, o:o + w]

        def vcol(name, j=0, n=1):
            return vec[:, VCOL[name] + j:VCOL[name] + j + n]

        ident, ones, bones = cst("ident"), cst("ones"), cst("bones")
        slot_loaded = [sem(f"slot_loaded{i}") for i in range(RING)]
        slot_used = [sem(f"slot_used{i}") for i in range(RING)]

        def slot(n, width=512, kts=KT):
            return ring[:, n % RING, 0:kts * width].rearrange("p (k n) -> p k n", k=kts)

        def wait_slot(eng, n):
            eng.wait_ge(slot_loaded[n % RING], 16 * (n // RING + 1))

        def free_slot(ins, n):
            ins.then_inc(slot_used[n % RING], 1)

        def load_slots(eng, first, last):
            for n in range(first, min(last, NSLOTS)):
                if n >= RING:
                    eng.wait_ge(slot_used[n % RING], n // RING)
                eng.dma_start(ring[:, n % RING, :], slots_in[n]).then_inc(slot_loaded[n % RING], 16)

        def after(name, part=None):
            o, w = SLOTS[name]
            return o + (w if part is None else part) + RING

        def done(eng, ins, s, value):
            ins.then_inc(s, 1)
            eng.wait_ge(s, value)

        class Chain:

            def __init__(self, eng, s):
                self.eng, self.s, self.n = eng, s, 0

            def __call__(self, ins):
                self.n += 1
                done(self.eng, ins, self.s, self.n)

        seq_v, seq_a, seq_g = sem("seq_v"), sem("seq_a"), sem("seq_g")
        chains = {}

        def chain(key, eng, s):
            if key not in chains:
                chains[key] = Chain(eng, s)
            chains[key].eng = eng
            return chains[key]

        GV = [(0, SLOTS[n][0] + i) for n in ("ada", "ada2", "ada3") for i in range(SLOTS[n][1])]
        GV += [(1, SLOTS["mod2"][0] + i) for i in range(12)]
        gv_row, gv_out, gv_col = sem("gv_row"), sem("gv_out"), sem("gv_col")
        mrow = area(ARENA - 512, 512)

        def pe_mod_row(pe, q):
            which, n = GV[q]
            wait_slot(pe, n)
            if q >= 2:
                pe.wait_ge(gv_out, q - 1)
            for k in range(KT):
                ins = pe.matmul(psum[5 + q % 2][0:1, :], csil[:, which, k:k + 1], slot(n)[:, k, :],
                                start=(k == 0), stop=(k == KT - 1))
            ins.then_inc(gv_row, 1)

        def pe_mod_cols(pe, q):
            pe.wait_ge(gv_out, q + 1)
            for m in range(4):
                col = 4 * (q % 12) + m
                ins = pe.matmul(psum[7][:, col:col + 1], mrow[0:1, m * P:(m + 1) * P], ones[0:1, 0:1],
                                start=True, stop=True)
            ins.then_inc(gv_col, 1)

        def act_mod_row(act, q):
            act.wait_ge(gv_row, q + 1)
            act.sem_inc(slot_used[GV[q][1] % RING], 1)
            if q:
                act.wait_ge(gv_col, q)
            act.copy(mrow[0:1, :], psum[5 + q % 2][0:1, :]).then_inc(gv_out, 1)

        def pe_mod(pe, first, last):
            for q in range(first, last):
                pe_mod_row(pe, q)
                if q > first:
                    pe_mod_cols(pe, q - 1)
            pe_mod_cols(pe, last - 1)

        c_ready, in_ready = sem("c_ready"), sem("in_ready")
        with nc.Block() as block:
            @block.sync
            def _(sp):
                sp.dma_start(vec[:], vecs_in).then_inc(in_ready, 16)
                load_slots(sp, 0, 2)
                sp.dma_start(con[:], consts_in).then_inc(in_ready, 16)
                sp.dma_start(xT[:], xT_in).then_inc(in_ready, 16)
                load_slots(sp, 2, after("ada"))

            @block.scalar
            def _(act):
                act.wait_ge(in_ready, 48)
                act.activation(csil[:, 0, :], vcol("c", 0, 8), ACT.Silu).then_inc(c_ready, 1)
                act.activation(csil[:, 1, :], vcol("c_2", 0, 8), ACT.Silu).then_inc(c_ready, 1)
                for q in range(4):
                    act_mod_row(act, q)

            @block.tensor
            def _(pe):
                pe.wait_ge(c_ready, 2)
                pe_mod(pe, 0, 4)

            @block.vector
            def _(dve):
                v = chain("v", dve, seq_v)
                for j, e in enumerate((RMS_EPS, LN_EPS, GN_EPS, 1.0)):
                    v(dve.memset(epsc[:, j:j + 1], e))
                dve.wait_ge(in_ready, 48)
                dve.wait_ge(gv_col, 4)
                v(dve.tensor_tensor(mod1[:, 0:16], psum[7][:, 0:16], vcol("ada_b", 0, 16), ALU.add))
                v(dve.scalar_tensor_tensor(gain[:, 0, :], mod1[:, 8:16], 1.0, vcol("norm_mix_g", 0, 8), ALU.add, ALU.mult))
        if STOP == "mod":
            return

        def norm_block(tag, gains, shifts, dst, then_load=None):
            sq_ready, ms_ready, sd_ready, n_ready = (sem(f"{tag}_{x}") for x in ("sq", "ms", "sd", "n"))
            sq = dst
            with nc.Block() as block:
                @block.scalar
                def _(act):
                    act.activation(sq[:, :, :], xT[:, :, :], ACT.Square).then_inc(sq_ready, 1)
                    act.wait_ge(ms_ready, 1)
                    act.activation(rstd[:], psum[0][:, 0:T], ACT.Sqrt, bias=epsc[:, 0:1],
                                   scale=1.0 / D).then_inc(sd_ready, 1)

                @block.tensor
                def _(pe):
                    pe.wait_ge(sq_ready, 1)
                    for k in range(KT):
                        ins = pe.matmul(psum[0][:, 0:T], ones, sq[:, k, :], start=(k == 0), stop=(k == KT - 1))
                    ins.then_inc(ms_ready, 1)

                @block.vector
                def _(dve):
                    v = chain("v", dve, seq_v)
                    dve.wait_ge(sd_ready, 1)
                    v(dve.reciprocal(rstd[:], rstd[:]))
                    for k in range(KT):
                        ins = dve.scalar_tensor_tensor(dst[:, k, :], xT[:, k, :], gains[:, k:k + 1], rstd[:],
                                                       ALU.mult, ALU.mult).then_inc(n_ready, 1)
                    if shifts is not None:
                        for k in range(KT):
                            dve.wait_ge(n_ready, k + 1)
                            dve.tensor_scalar(dst[:, k, :], dst[:, k, :], shifts[:, k:k + 1], None, ALU.add)

        norm_block("mix", gain[:, 0, :], mod1[:, 0:8], uT)
        if STOP == "norm1":
            return

        pB = area(0, NPROJ, T + 1)
        xs = area(3598, NPROJ, T)
        ypad = area(7182, CT, TAPS - 1 + T)

        def pe_project(pe, name, tiles, rhs, mm, ev, base=0, banks=8, width=512, kts=KT, sl=None):
            s0, _ = SLOTS[name]
            for i, (s, col) in enumerate(tiles):
                if i == 0 or tiles[i - 1][0] != s:
                    wait_slot(pe, s0 + s)
                if i >= banks:
                    pe.wait_ge(ev, i - banks + 1)
                for k in range(kts):
                    ins = pe.matmul(psum[base + i % banks][:, 0:T], slot(s0 + s, width, kts)[:, k, col:col + P],
                                    rhs[:, k, :], start=(k == 0), stop=(k == kts - 1))
                ins.then_inc(mm, 1)

        in_mm, in_ev, in_zero, in_glu = sem("in_mm"), sem("in_ev"), sem("in_zero"), sem("in_glu")
        w_in_tiles = [(i // 4, (i % 4) * P) for i in range(22)]
        sqc = area(8960, CT, T)
        mean, var = area(9984, T), area(10240, T)
        cv_acc, cv_sq, cv_mm, cv_sd, cv_out = (sem(f"cv_{x}") for x in ("acc", "sq", "mm", "sd", "out"))
        with nc.Block() as block:
            @block.sync
            def _(sp):
                load_slots(sp, after("ada"), after("ada2"))

            @block.gpsimd
            def _(pool):
                pool.memset(pB[:, :, 0:1], 0.0).then_inc(in_zero, 1)
                pool.memset(ypad[:, :, 0:TAPS - 1], 0.0).then_inc(in_zero, 1)

            @block.tensor
            def _(pe):
                pe_project(pe, "w_in", w_in_tiles, uT, in_mm, in_ev, banks=5)
                pe_mod(pe, 4, 6)
                pe.wait_ge(cv_acc, TAPS * CT)
                for ct in range(CT):
                    ins = pe.matmul(psum[0][:, 0:T], ones, mixT[:, ct, :], start=(ct == 0), stop=(ct == CT - 1))
                ins.then_inc(cv_mm, 1)
                pe.wait_ge(cv_sq, 1)
                for ct in range(CT):
                    ins = pe.matmul(psum[1][:, 0:T], ones, sqc[:, ct, :], start=(ct == 0), stop=(ct == CT - 1))
                ins.then_inc(cv_mm, 1)

            @block.scalar
            def _(act):
                s0 = SLOTS["w_in"][0]
                for i in range(22):
                    act.wait_ge(in_mm, i + 1)
                    src = psum[i % 5][:, 0:T]
                    if i % 4 == 3 or i == 21:
                        act.sem_inc(slot_used[(s0 + i // 4) % RING], 1)
                    if i < 4:
                        ins = act.copy(ypad[:, i, TAPS - 1:], src)
                    elif i < 8:
                        ins = act.activation(mixT[:, i - 4, :], src, ACT.Sigmoid)
                    else:
                        ins = act.copy(pB[:, i - 8, 1:], src)
                    ins.then_inc(in_ev, 1)
                for q in (4, 5):
                    act_mod_row(act, q)
                act.wait_ge(cv_acc, TAPS * CT + CT)
                act.activation(sqc, mixT[:, 0:CT, :], ACT.Square).then_inc(cv_sq, 1)
                act.wait_ge(cv_mm, 2)
                act.activation(var, psum[1][:, 0:T], ACT.Sqrt, bias=epsc[:, 1:2], scale=1.0 / CH).then_inc(cv_sd, 1)
                act.wait_ge(cv_out, CT)
                act.activation(mixT[:, 0:CT, :], mixT[:, 0:CT, :], ACT.Silu).then_inc(seq_a, 1)

            @block.vector
            def _(dve):
                v = chain("v", dve, seq_v)
                dve.wait_ge(in_zero, 2)
                for i in range(CT):
                    dve.wait_ge(in_ev, 5 + i)
                    dve.tensor_tensor(ypad[:, i, TAPS - 1:], ypad[:, i, TAPS - 1:], mixT[:, i, :], ALU.mult).then_inc(in_glu, 1)
                for j in range(TAPS):
                    for ct in range(CT):
                        n = j * CT + ct
                        src, wc = ypad[:, ct, j:j + T], vcol("conv_dw_w", n)
                        if j == 0:
                            dve.wait_ge(in_glu, ct + 1)
                            ins = dve.tensor_scalar(mixT[:, ct, :], src, wc, vcol("conv_dw_b", ct), ALU.mult, ALU.add)
                        else:
                            dve.wait_ge(cv_acc, n - CT + 1)
                            ins = dve.scalar_tensor_tensor(mixT[:, ct, :], src, wc, mixT[:, ct, :], ALU.mult, ALU.add)
                        ins.then_inc(cv_acc, 1)
                dve.wait_ge(in_ev, 22)
                dve.wait_ge(cv_mm, 1)
                v(dve.tensor_scalar(mean, psum[0][:, 0:T], 1.0 / CH, None, ALU.mult))
                for ct in range(CT):
                    dve.tensor_tensor(mixT[:, ct, :], mixT[:, ct, :], mean, ALU.subtract).then_inc(cv_acc, 1)
                dve.tensor_tensor(xs, pB[:, :, 0:T], pB[:, :, 1:T + 1], ALU.subtract)
                dve.wait_ge(cv_sd, 1)
                v(dve.reciprocal(var, var))
                for ct in range(CT):
                    dve.wait_ge(cv_acc, TAPS * CT + ct + 1)
                    v(dve.scalar_tensor_tensor(mixT[:, ct, :], mixT[:, ct, :], vcol("conv_ln_w", ct), var,
                                               ALU.mult, ALU.mult))
                    dve.tensor_scalar(mixT[:, ct, :], mixT[:, ct, :], vcol("conv_ln_b", ct), None,
                                      ALU.add).then_inc(cv_out, 1)
        if STOP == "conv":
            return

        B0 = 8960
        BDk, BDb, BDc, BDr, BDv = (area(B0 + i * 2048, CT, NC, 2, C) for i in range(5))
        RH = area(B0 + 10240, CT, NC, 2, C)
        bS = area(B0 + 12288, CT, NC, C)
        gate = area(B0 + 13312, CT, T)
        bv = area(B0 + 14336, CT, T)
        dec = area(B0 + 15360, CT, NC, C + 1)
        T0 = area(B0 + 16400, CT, T)
        T1 = area(B0 + 17424, CT, T)
        T2, T3, T4 = uT[:, 0:4, :], uT[:, 4:8, :], mixT[:, 4:8, :]
        th = area(B0 + 18448, T)
        sg = area(B0 + 18704, T)
        assert B0 + 18960 <= ARENA

        def by_chunk(a):
            return a.rearrange("p c (n t) -> p c n t", n=NC)

        rw = {x: sem("rw_" + x) for x in ("zero", "xs", "th", "sg", "lora", "sigw", "a", "g", "ld", "L", "D", "sq",
                                          "ss", "nrm", "kap", "bs", "ks", "rs", "rk", "bonus", "gout")}
        with nc.Block() as block:
            @block.sync
            def _(sp):
                load_slots(sp, after("ada2"), after("ada3"))

            @block.gpsimd
            def _(pool):
                g = chain("g", pool, seq_g)
                for b in (BDk, BDb, BDc, BDr, BDv):
                    g(pool.memset(b[0:64, :, :, 1, :], 0.0))
                    g(pool.memset(b[64:128, :, :, 0, :], 0.0))
                pool.memset(dec[:, :, :, 0:1], 1.0).then_inc(rw["zero"], 1)
                pool.wait_ge(rw["xs"], NPROJ)
                for hh in range(2):
                    s = slice(64 * hh, 64 * hh + 64)
                    g(pool.tensor_copy(BDv[s, :, :, hh, :], by_chunk(xs[s, 8:12, :])))

            @block.vector
            def _(dve):
                v = chain("v", dve, seq_v)
                for i in (12, 13, *range(12)):
                    dve.scalar_tensor_tensor(xs[:, i, :], xs[:, i, :], vcol("rwkv_mu", i), pB[:, i, 1:T + 1],
                                             ALU.mult, ALU.add).then_inc(rw["xs"], 1)
                dve.wait_ge(rw["xs"], NPROJ)
                r, k = xs[:, 0:4, :], xs[:, 4:8, :]
                for ct in range(CT):
                    ins = dve.tensor_scalar(T4[:, ct, :], k[:, ct, :], vcol("rwkv_k_k", ct), None, ALU.mult)
                    v(ins)
                dve.tensor_tensor(bv, T4, T4, ALU.mult).then_inc(rw["sq"], 1)
                dve.wait_ge(rw["sigw"], CT)
                v(dve.tensor_scalar(T2, T0, -float(np.exp(np.float64(-0.5))), None, ALU.mult))
                for ct in range(CT):
                    dve.tensor_tensor_scan(T3[:, ct, :], cst("chunk"), T2[:, ct, :], 0.0, ALU.mult,
                                           ALU.add).then_inc(rw["L"], 1)
                dve.wait_ge(rw["a"], CT)
                dve.wait_ge(rw["L"], CT)
                for ct in range(CT):
                    v(dve.tensor_scalar(T0[:, ct, :], T1[:, ct, :], -1.0, vcol("rwkv_k_a", ct), ALU.add, ALU.mult))
                v(dve.scalar_tensor_tensor(T0, T0, 1.0, k, ALU.add, ALU.mult))
                for ct in range(CT):
                    v(dve.tensor_scalar(T2[:, ct, :], r[:, ct, :], vcol("rwkv_r_k", ct), None, ALU.mult))
                dve.tensor_tensor(T2, T2, T0, ALU.mult).then_inc(rw["rk"], 1)
                dve.wait_ge(rw["nrm"], 2)
                v(dve.tensor_scalar(bv, bv, 1e-12, None, ALU.max))
                v(dve.reciprocal(bv, bv))
                v(dve.tensor_tensor(T4, T4, bv, ALU.mult))
                v(dve.tensor_tensor(T1, T1, T4, ALU.mult))
                dve.wait_ge(rw["D"], 2 * CT)
                dve.wait_ge(rw["zero"], 1)
                for ct in range(CT):
                    dve.tensor_tensor(RH[:, ct, :, 0, :], by_chunk(T4)[:, ct], dec[:, ct, :, 0:C], ALU.mult).then_inc(rw["kap"], 1)
                    dve.tensor_tensor(RH[:, ct, :, 1, :], by_chunk(r)[:, ct], dec[:, ct, :, 1:], ALU.mult).then_inc(rw["rs"], 1)
                dve.tensor_tensor(bS.rearrange("p a b c -> p a (b c)"), T1, T3, ALU.mult).then_inc(rw["bs"], 1)
                v(dve.tensor_tensor(T0, T0, T3, ALU.mult))
                for hh in range(2):
                    s = slice(64 * hh, 64 * hh + 64)
                    dve.tensor_copy(BDk[s, :, :, hh, :], by_chunk(T0[s]))
                dve.wait_ge(rw["bonus"], 2)
                for h in range(2):
                    dve.tensor_tensor(bv[:, 2 * h:2 * h + 2, :], psum[3 + h][:, :].rearrange("p (c t) -> p c t", c=2),
                                      xs[:, 8 + 2 * h:10 + 2 * h, :], ALU.mult)

            @block.scalar
            def _(act):
                act.wait_ge(rw["xs"], 2)
                act.activation(th[0:64], xs[0:64, 12, :], ACT.Tanh).then_inc(rw["th"], 1)
                act.activation(sg, xs[:, 13, :], ACT.Sigmoid).then_inc(rw["sg"], 1)
                for ct in range(CT):
                    act.wait_ge(rw["lora"], ct // 2 + 1)
                    col = slice((ct % 2) * T, (ct % 2 + 1) * T)
                    act.activation(T0[:, ct, :], psum[ct // 2][:, col], ACT.Sigmoid,
                                   bias=vcol("rwkv_w0", ct)).then_inc(rw["sigw"], 1)
                    act.activation(T1[:, ct, :], psum[2 + ct // 2][:, col], ACT.Sigmoid,
                                   bias=vcol("rwkv_a0", ct)).then_inc(rw["a"], 1)
                for h in range(2):
                    act.wait_ge(rw["g"], h + 1)
                    act.copy(gate[:, 2 * h:2 * h + 2, :], psum[4 - 4 * h][:, :].rearrange("p (c t) -> p c t", c=2)
                             ).then_inc(rw["gout"], 1)
                act_mod_row(act, 6)
                for h in range(2):
                    act.wait_ge(rw["ss"], h + 1)
                    act.activation(bv[:, 2 * h:2 * h + 2, :], psum[1 + h][:, :].rearrange("p (c t) -> p c t", c=2),
                                   ACT.Sqrt).then_inc(rw["nrm"], 1)
                act.wait_ge(rw["zero"], 1)
                for sign in (1, -1):
                    for ct in range(CT):
                        act.wait_ge(rw["L"], ct + 1)
                        if sign < 0:
                            act.wait_ge(rw["D"], ct + 1)
                        act.activation(dec[:, ct, :, 1:] if sign > 0 else by_chunk(T3)[:, ct], by_chunk(T3)[:, ct],
                                       ACT.Exp, scale=float(sign)).then_inc(rw["D"], 1)
                act_mod_row(act, 7)
                act_mod_row(act, 8)
                act.wait_ge(rw["kap"], CT)
                act.wait_ge(rw["rs"], CT)
                act.wait_ge(rw["bs"], 1)
                for hh in range(2):
                    s = slice(64 * hh, 64 * hh + 64)
                    act.copy(BDc[s, :, :, hh, :], RH[s, :, :, 0, :])
                    act.copy(BDr[s, :, :, hh, :], RH[s, :, :, 1, :])
                    act.copy(BDb[s, :, :, hh, :], bS[s])
                for q in (9, 10, 11):
                    act_mod_row(act, q)

            @block.tensor
            def _(pe):
                n = SLOTS["lora"][0]
                wait_slot(pe, n)
                lora = ring[:, n % RING, :]
                pe.wait_ge(rw["th"], 1)
                pe.wait_ge(rw["sg"], 1)
                def col(ct):
                    return slice((ct % 2) * T, (ct % 2 + 1) * T)

                for ct in range(CT):
                    wc = slice(ct * P, ct * P + P)
                    pe.matmul(psum[ct // 2][:, col(ct)], lora[0:64, wc], th[0:64], start=True, stop=True)
                    ins = pe.matmul(psum[2 + ct // 2][:, col(ct)], lora[64:128, wc], xs[64:128, 12, :], start=True, stop=True)
                    if ct % 2:
                        ins.then_inc(rw["lora"], 1)
                for h in range(2):
                    if h:
                        pe.wait_ge(rw["sigw"], 2)
                    for ct in (2 * h, 2 * h + 1):
                        ins = pe.matmul(psum[4 - 4 * h][:, col(ct)], lora[:, CH + ct * P:CH + ct * P + P], sg,
                                        start=True, stop=True)
                    ins.then_inc(rw["g"], 1)
                pe_mod_row(pe, 6)
                pe.wait_ge(rw["g"], 2)
                pe.sem_inc(slot_used[n % RING], 1)
                pe.wait_ge(rw["sq"], 1)
                pe.wait_ge(rw["sigw"], CT)
                pe.wait_ge(rw["a"], 2)
                for ct in range(CT):
                    ins = pe.matmul(psum[1 + ct // 2][:, col(ct)], bones, bv[:, ct, :], start=True, stop=True)
                    if ct % 2:
                        ins.then_inc(rw["ss"], 1)
                pe_mod_cols(pe, 6)
                pe_mod_row(pe, 7)
                pe.wait_ge(rw["rk"], 1)
                pe.wait_ge(rw["a"], CT)
                pe.wait_ge(rw["gout"], 1)
                for ct in range(CT):
                    ins = pe.matmul(psum[3 + ct // 2][:, col(ct)], bones, T2[:, ct, :], start=True, stop=True)
                    if ct % 2:
                        ins.then_inc(rw["bonus"], 1)
                pe_mod_cols(pe, 7)
                pe_mod(pe, 8, 12)
        if STOP == "prep":
            return

        def bdm(at):
            return area(at, CT, P)
        names = ["Po", "Q", "QT", "N", "RB", "RK", "tb", "tk"]
        mat = {n: bdm(i * 512) for i, n in enumerate(names)}
        RP, WM = ([area(4608 + (2 * j + i) * 1024, CT, 2, P) for j in range(2)] for i in range(2))
        Ss = area(4096, CT, C)
        Vs = area(4352, CT, C)
        Us = area(B0 + 18448, CT, C)
        Rn = area(B0 + 18704, CT, C)
        st = area(B0 + 18960, 3, NC, CT)
        yT = T0
        Ybd = uT[:, :, :].rearrange("p a (d x) -> p (a d) x", d=2).rearrange("p (c e) x -> p c e x", c=NC)
        yn = area(B0 + 17424, NC, CT, C)
        sq = area(512, NC, CT, C)
        rc_mm, rc_ev, rc_zero, rc_half, rc_sum, rc_var, rc_sd = (sem(f"rc_{x}") for x in ("mm", "ev", "zero", "half", "sum", "var", "sd"))

        def two(bank, n=P):
            return psum[bank][:, 0:2 * n].rearrange("p (c x) -> p c x", c=2)

        class Steps:
            (G1, G3, G2, TV, P2, M2, TB, TK, L1R, L1W, L2R, L2W, L3R, L3W, RN, Q_, QT_, Z_, Q2T, Y_, U_, S_,
             Y) = range(23)
            COUNT = 2 * 23
        S = Steps
        NEEDS = {S.P2: S.G3, S.M2: S.G3, S.L1R: S.M2, S.L1W: S.M2, S.L2R: S.L1W, S.L2W: S.L1W, S.L3R: S.L2W,
                 S.L3W: S.L2W, S.Q_: S.L3W, S.QT_: S.L3W, S.Z_: S.QT_, S.Q2T: S.QT_, S.Y_: S.Q2T, S.RN: S.TV,
                 S.U_: S.Y_, S.S_: S.U_, S.Y: S.U_}
        HALVES = (0, 1)
        with nc.Block() as block:
            @block.gpsimd
            def _(pool):
                g = chain("g", pool, seq_g)
                for n in names:
                    if n not in ("tb", "tk"):
                        g(pool.memset(mat[n][0:64, :, C:P], 0.0))
                        g(pool.memset(mat[n][64:128, :, 0:C], 0.0))
                for a in (RP[0][:, :, 0, :], WM[0][:, :, 0, :], RP[1][:, :, 1, :], WM[1][:, :, 1, :]):
                    g(pool.memset(a[0:64, :, C:P], 0.0))
                    g(pool.memset(a[64:128, :, 0:C], 0.0))
                g(pool.memset(Ybd, 0.0))
                pool.memset(Ss, 0.0).then_inc(rc_zero, 1)

            @block.tensor
            def _(pe):
                pe.wait_ge(rc_zero, 1)
                for c in range(NC):
                    base = c * S.COUNT

                    def begin(k, h):
                        n = base + 2 * k + h
                        need = max(n - 6, base + 2 * NEEDS[k] + h + 1 if k in NEEDS else 0, 0)
                        if need > 0:
                            pe.wait_ge(rc_ev, need)
                        return n % 7

                    def products(k, terms, n=P):
                        for h in HALVES:
                            b = begin(k, h)
                            for j in range(2):
                                for i, (l, r_) in enumerate(terms):
                                    ins = pe.matmul(psum[b][:, j * n:(j + 1) * n], l(2 * h + j), r_(2 * h + j),
                                                    start=(i == 0), stop=(i == len(terms) - 1))
                            ins.then_inc(rc_mm, 1)

                    def flip(k, src):
                        for h in HALVES:
                            b = begin(k, h)
                            for j in range(2):
                                ins = pe.transpose(psum[b][:, j * P:(j + 1) * P], src(2 * h + j), ident)
                            ins.then_inc(rc_mm, 1)

                    def both(a):
                        return lambda ct: a[:, ct].rearrange("p a x -> p (a x)")

                    def part(a, i):
                        return lambda ct: a[:, ct, i, :]

                    def bd(a):
                        return lambda ct: a[:, ct, c].rearrange("p h t -> p (h t)")

                    def m(name):
                        return lambda ct: mat[name][:, ct, :]

                    def rh(lo, hi):
                        return lambda ct: RH[:, ct, c, lo:hi, :].rearrange("p a t -> p (a t)")
                    products(S.G1, [(bd(BDb), rh(0, 2))])
                    products(S.G3, [(bd(BDc), lambda ct: bS[:, ct, c, :])], C)
                    products(S.G2, [(bd(BDk), rh(0, 2))])
                    flip(S.TV, bd(BDv))
                    products(S.P2, [(part(WM[1], 1), part(RP[1], 1))])
                    products(S.M2, [(part(RP[1], 1), part(WM[1], 1))])
                    flip(S.TB, bd(BDb))
                    flip(S.TK, bd(BDk))
                    for old, (k, kw) in enumerate(((S.L1R, S.L1W), (S.L2R, S.L2W))):
                        products(k, [(part(WM[old], 1), both(RP[old]))], 2 * P)
                        products(kw, [(part(RP[old], 1), both(WM[old]))], 2 * P)
                    products(S.L3R, [(part(WM[0], 1), part(RP[0], 0))])
                    products(S.L3W, [(part(RP[0], 1), part(WM[0], 0))])
                    products(S.RN, [(bd(BDc), lambda ct: Ss[:, ct, :]), (m("N"), lambda ct: Vs[:, ct, :])], C)
                    products(S.Q_, [(part(WM[1], 0), m("Po"))])
                    products(S.QT_, [(m("Po"), part(WM[1], 0))])
                    products(S.Z_, [(m("QT"), part(RP[1], 0))])
                    products(S.Q2T, [(m("Q"), m("QT"))])
                    products(S.Y_, [(m("Po"), part(RP[0], 0))])
                    products(S.U_, [(part(RP[1], 0), lambda ct: Rn[:, ct, :])], C)
                    products(S.S_, [(m("tb"), lambda ct: Us[:, ct, :]), (m("tk"), lambda ct: Vs[:, ct, :])], C)
                    products(S.Y, [(bd(BDr), lambda ct: Ss[:, ct, :]), (m("RB"), lambda ct: Us[:, ct, :]),
                                   (m("RK"), lambda ct: Vs[:, ct, :])], C)
                for c in range(NC):
                    pe.wait_ge(rc_ev, NC * S.COUNT + c + 1)
                    for ct in range(CT):
                        ins = pe.transpose(psum[c][:, ct * P:(ct + 1) * P], Ybd[:, c, ct, :], ident)
                    ins.then_inc(rc_mm, 1)

            @block.vector
            def _(dve):
                v = chain("v", dve, seq_v)
                dve.wait_ge(rc_zero, 1)
                halves = [0]
                H = (slice(0, 64), slice(64, 128))
                for c in range(NC):
                    base = c * S.COUNT

                    def begin(k, h):
                        dve.wait_ge(rc_mm, base + 2 * k + h + 1)
                        return (base + 2 * k + h) % 7

                    def tiles(h):
                        return slice(2 * h, 2 * h + 2)

                    def masked(dst, bank, h, head, mask, width=P, off=0):
                        s = H[head]
                        return dve.tensor_tensor(dst[s, tiles(h), head * C:head * C + C], two(bank, width)[s, :, off:off + C],
                                                 cst(mask)[s].unsqueeze(1).to_broadcast([64, 2, C]), ALU.mult)

                    def last(ins):
                        ins.then_inc(rc_ev, 1)

                    def copy(k, dst):
                        for h in HALVES:
                            last(dve.tensor_copy(dst[:, tiles(h)], two(begin(k, h))))

                    def combine(k, dst, a, op):
                        for h in HALVES:
                            last(dve.tensor_tensor(dst[:, tiles(h)], a[:, tiles(h)], two(begin(k, h)), op))

                    def first_power(k, pw, sm, mask, width):
                        for h in HALVES:
                            b = begin(k, h)
                            for head in range(2):
                                masked(pw, b, h, head, mask, width).then_inc(rc_half, 1)
                            if k == S.G1:
                                for head in range(2):
                                    masked(mat["Po"], b, h, head, "oS")
                                    masked(mat["RB"], b, h, head, "mI", off=C)
                            for head in range(2):
                                s = H[head]
                                halves[0] += 1
                                dve.wait_ge(rc_half, halves[0])
                                ins = dve.tensor_tensor(sm[s, tiles(h), head * C:head * C + C],
                                                        cst("eye")[s].unsqueeze(1).to_broadcast([64, 2, C]),
                                                        pw[s, tiles(h), head * C:head * C + C], ALU.subtract)
                            last(ins)

                    first_power(S.G1, RP[1][:, :, 1, :], RP[0][:, :, 0, :], "dS", P)
                    first_power(S.G3, WM[1][:, :, 1, :], WM[0][:, :, 0, :], "dL", C)
                    for h in HALVES:
                        b = begin(S.G2, h)
                        for head in range(2):
                            masked(mat["RK"], b, h, head, "mI", off=C)
                            ins = masked(mat["N"], b, h, head, "mS")
                        last(ins)
                    for h in HALVES:
                        b = begin(S.TV, h)
                        for head in range(2):
                            ins = dve.tensor_copy(Vs[H[head], tiles(h)], two(b)[H[head], :, head * C:head * C + C])
                        last(ins)
                    copy(S.P2, RP[0][:, :, 1, :])
                    copy(S.M2, WM[0][:, :, 1, :])
                    copy(S.TB, mat["tb"])
                    copy(S.TK, mat["tk"])
                    for k, a, old in ((S.L1R, RP, 0), (S.L1W, WM, 0), (S.L2R, RP, 1), (S.L2W, WM, 1)):
                        for h in HALVES:
                            b = psum[begin(k, h)][:, :].rearrange("p (c a x) -> p c a x", c=2, a=2)
                            dve.tensor_copy(a[1 - old][:, tiles(h), 1, :], b[:, :, 1, :])
                            last(dve.tensor_tensor(a[1 - old][:, tiles(h), 0, :], a[old][:, tiles(h), 0, :],
                                                   b[:, :, 0, :], ALU.add))
                    combine(S.L3R, RP[1][:, :, 0, :], RP[0][:, :, 0, :], ALU.add)
                    combine(S.L3W, WM[1][:, :, 0, :], WM[0][:, :, 0, :], ALU.add)
                    for h in HALVES:
                        last(dve.tensor_scalar(Rn[:, tiles(h)], two(begin(S.RN, h), C), -1.0, None, ALU.mult))
                    copy(S.Q_, mat["Q"])
                    copy(S.QT_, mat["QT"])
                    combine(S.Z_, RP[0][:, :, 0, :], RP[1][:, :, 0, :], ALU.subtract)
                    copy(S.Q2T, mat["Po"])
                    combine(S.Y_, RP[1][:, :, 0, :], RP[0][:, :, 0, :], ALU.add)
                    for h in HALVES:
                        last(dve.tensor_copy(Us[:, tiles(h)], two(begin(S.U_, h), C)))
                    banks = [begin(S.S_, h) for h in HALVES]
                    ybanks = [begin(S.Y, h) for h in HALVES]
                    for h in HALVES:
                        dve.tensor_tensor(Ss[:, tiles(h)], Ss[:, tiles(h)], two(banks[h], C), ALU.add).then_inc(rc_sum, 1)
                    for h in HALVES:
                        dve.wait_ge(rc_sum, 2 * c + h + 1)
                        last(dve.tensor_tensor(Ss[:, tiles(h)], Ss[:, tiles(h)],
                                               dec[:, tiles(h), c, C:C + 1].to_broadcast([P, 2, C]), ALU.mult))
                    for h in HALVES:
                        last(dve.tensor_copy(yn[:, c, tiles(h)], two(ybanks[h], C)))
                dve.wait_ge(rc_ev, NC * S.COUNT)
                bc = [P, NC * CT, C]
                flat = lambda a: a.rearrange("p n c i -> p (n c) i")
                mu, vr, sd = (st[:, i].rearrange("p n c -> p (n c)") for i in range(3))
                v(dve.tensor_reduce(mu, flat(yn), AX_X, ALU.add))
                v(dve.tensor_scalar(mu, mu, 1.0 / C, None, ALU.mult))
                v(dve.tensor_tensor(flat(yn), flat(yn), mu.unsqueeze(2).to_broadcast(bc), ALU.subtract))
                v(dve.tensor_tensor(flat(sq), flat(yn), flat(yn), ALU.mult))
                v(dve.tensor_reduce(vr, flat(sq), AX_X, ALU.add))
                v(dve.tensor_scalar(vr, vr, 1.0 / C, GN_EPS, ALU.mult, ALU.add))
                dve.reciprocal(vr, vr).then_inc(rc_var, 1)
                dve.wait_ge(rc_sd, 1)
                for c in range(NC):
                    for h in range(2):
                        ins = dve.tensor_tensor(Ybd[H[h], c, :, h * C:h * C + C], yn[H[h], c],
                                                st[H[h], 2, c].unsqueeze(2).to_broadcast([64, CT, C]), ALU.mult)
                    last(ins)
                for c in range(NC):
                    dve.wait_ge(rc_mm, NC * S.COUNT + c + 1)
                    y = psum[c][:, :].rearrange("p (c x) -> p c x", c=CT)
                    for h in range(2):
                        ins = dve.tensor_copy(yT[H[h], :, c * C:c * C + C], y[H[h], :, h * C:h * C + C])
                    last(ins)
                dve.wait_ge(rc_ev, NC * (S.COUNT + 2))
                for ct in range(CT):
                    v(dve.tensor_scalar(yT[:, ct, :], yT[:, ct, :], vcol("rwkv_gn_w", ct), vcol("rwkv_gn_b", ct),
                                        ALU.mult, ALU.add))
                v(dve.tensor_tensor(yT, yT, bv, ALU.add))
                v(dve.tensor_tensor(mixT[:, 4:8, :], yT, gate, ALU.mult))
                v(dve.tensor_tensor(mod1[:, 16:48], psum[7][:, 16:48], vcol("ada_b", 16, 32), ALU.add))
                v(dve.scalar_tensor_tensor(gain[:, 1, :], mod1[:, 32:40], 1.0, vcol("norm_ffn_g", 0, 8), ALU.add, ALU.mult))

            @block.scalar
            def _(act):
                act.wait_ge(rc_var, 1)
                act.activation(st[:, 2], st[:, 1], ACT.Sqrt).then_inc(rc_sd, 1)
        if STOP == "rwkv":
            return

        def residual_block(tag, name, tiles, rhs, gates, load, width=512, kts=KT, mm_fn=None):
            mm, ev = sem(tag + "_mm"), sem(tag + "_ev")
            with nc.Block() as block:
                @block.sync
                def _(sp):
                    load_slots(sp, *load)

                @block.tensor
                def _(pe):
                    pe_project(pe, name, tiles, rhs, mm, ev, width=width, kts=kts)

                @block.vector
                def _(dve):
                    s0 = SLOTS[name][0]
                    for i, (s, _) in enumerate(tiles):
                        dve.wait_ge(mm, i + 1)
                        dve.scalar_tensor_tensor(xT[:, i, :], psum[i % 8][:, 0:T], gates[:, i:i + 1], xT[:, i, :],
                                                 ALU.mult, ALU.add).then_inc(ev, 1)
                        if i == len(tiles) - 1 or tiles[i + 1][0] != s:
                            dve.sem_inc(slot_used[(s0 + s) % RING], 1)

        eight = [(i // 4, (i % 4) * P) for i in range(8)]
        residual_block("o1", "w_out", eight, mixT, mod1[:, 16:24], (after("ada3"), after("w_out")))
        if STOP == "w_out":
            return
        norm_block("ffn", gain[:, 1, :], mod1[:, 24:32], uT)

        NHP = 2 * HEADS
        qT = area(0, NHP, T)
        utok = area(4096, TT, D)
        wq_mm, wq_ev, ut_mm, ut_ev = sem("wq_mm"), sem("wq_ev"), sem("ut_mm"), sem("ut_ev")
        with nc.Block() as block:
            @block.sync
            def _(sp):
                load_slots(sp, after("w_out"), after("w_q"))

            @block.tensor
            def _(pe):
                for tt in range(TT):
                    for h in range(2):
                        for j in range(4):
                            ins = pe.transpose(psum[4 + 2 * tt + h][:, j * P:(j + 1) * P],
                                               uT[:, 4 * h + j, tt * P:(tt + 1) * P], ident)
                        ins.then_inc(ut_mm, 1)
                pe_project(pe, "w_q", [(i // 4, (i % 4) * P) for i in range(NHP)], uT, wq_mm, wq_ev, banks=4)

            @block.scalar
            def _(act):
                for tt in range(TT):
                    for h in range(2):
                        act.wait_ge(ut_mm, 2 * tt + h + 1)
                        act.copy(utok[:, tt, 512 * h:512 * h + 512], psum[4 + 2 * tt + h][:, :])
                s0 = SLOTS["w_q"][0]
                for i in range(NHP):
                    act.wait_ge(wq_mm, i + 1)
                    if i % 4 == 3:
                        act.sem_inc(slot_used[(s0 + i // 4) % RING], 1)
                    act.copy(qT[:, i, :], psum[i % 4][:, 0:T]).then_inc(wq_ev, 1)

        top = area(6144, TT, NHP, TOPK)
        topi = area(6656, TT, NHP, TOPK)
        topu = area(7168, TT, NHP, TOPK).bitcast(U32)
        work = area(7680, 8, P)
        keys = area(17000, NHP, NKEYS)
        cand = area(8704, HEADS, TOPK * TOPK)
        cwork = area(10752, HEADS, TOPK * TOPK)
        best = area(12800, TT, HEADS, TOPK)
        posu = area(13056, TT, HEADS, TOPK).bitcast(U32)
        half_u = area(13312, HEADS, TOPK).bitcast(U32)
        half_f = area(13440, HEADS, TOPK)
        pick = area(13568, 2, HEADS, TOPK)
        hot = area(13824, HEADS, TOPK, TOPK)
        prob = area(15872, TT, HEADS, TOPK)
        expert = area(16128, TT, NSEL).bitcast(U32)
        den = area(16384, TT, HEADS)
        best0 = area(16400, TT, HEADS, TOPK)
        keys_out, sc_mm, sc_used, tk_ready, tk_best, tk_exp = (sem(x) for x in ("keys_out", "sc_mm", "sc_used", "tk_ready", "tk_best", "tk_exp"))
        with nc.Block() as block:
            @block.sync
            def _(sp):
                load_slots(sp, after("w_q"), after("mod2"))

            @block.tensor
            def _(pe):
                pe.wait_ge(keys_out, 1)
                q = 12
                for g in range(2 * CT):
                    if g >= 5:
                        pe.wait_ge(sc_used, g - 4)
                        for _ in range(4):
                            pe_mod_row(pe, q)
                            pe_mod_cols(pe, q)
                            q += 1
                    tt = g // 4
                    for j in range(4):
                        hp = 4 * (g % 4) + j
                        ins = pe.matmul(psum[g % 5][:, j * P:(j + 1) * P], qT[:, hp, tt * P:(tt + 1) * P],
                                        keys[:, hp, :], start=True, stop=True)
                    ins.then_inc(sc_mm, 1)

            @block.vector
            def _(dve):
                v = chain("v", dve, seq_v)
                count = [0]

                def lanes(ops, n):
                    for op in ops:
                        for j in range(n):
                            if op is not ops[0]:
                                dve.wait_ge(tk_ready, count[0] - n + 1)
                            op(j).then_inc(tk_ready, 1)
                            count[0] += 1
                    dve.wait_ge(tk_ready, count[0])

                def top16(src, wrk, vals, inds, n):
                    lanes([lambda j: dve.max(vals(j)[:, 0:8], src(j)),
                           lambda j: dve.max_index(inds(j)[:, 0:8], vals(j)[:, 0:8], src(j)),
                           lambda j: dve.match_replace(wrk(j), vals(j)[:, 0:8], src(j), TAKEN),
                           lambda j: dve.max(vals(j)[:, 8:16], wrk(j)),
                           lambda j: dve.max_index(inds(j)[:, 8:16], vals(j)[:, 8:16], wrk(j))], n)

                for tt in range(TT):
                    for g in range(4):
                        dve.wait_ge(sc_mm, 4 * tt + g + 1)
                        top16(lambda j: psum[(4 * tt + g) % 5][:, j * P:(j + 1) * P], lambda j: work[:, j, :],
                              lambda j: top[:, tt, 4 * g + j, :], lambda j: topu[:, tt, 4 * g + j, :], 4)
                        dve.sem_inc(sc_used, 1)
                    v(dve.tensor_copy(topi[:, tt], topu[:, tt]))
                    bc = [P, HEADS, TOPK, TOPK]
                    v(dve.tensor_tensor(cand.rearrange("p h (a b) -> p h a b", a=TOPK),
                                        top[:, tt, 0::2, :].unsqueeze(3).to_broadcast(bc),
                                        top[:, tt, 1::2, :].unsqueeze(2).to_broadcast(bc), ALU.add))
                    top16(lambda j: cand[:, j, :], lambda j: cwork[:, j, :], lambda j: best[:, tt, j, :],
                          lambda j: posu[:, tt, j, :], HEADS)
                    dve.tensor_tensor(best0[:, tt], best[:, tt], best[:, tt, :, 0:1].to_broadcast([P, HEADS, TOPK]),
                                      ALU.subtract).then_inc(tk_best, 1)
                    for half, (op, by) in enumerate(((ALU.logical_shift_right, 4), (ALU.bitwise_and, 15))):
                        v(dve.tensor_scalar(half_u, posu[:, tt], by, None, op))
                        v(dve.tensor_copy(half_f, half_u))
                        v(dve.tensor_tensor(hot, half_f.unsqueeze(3).to_broadcast(bc),
                                            cst("iota").unsqueeze(1).unsqueeze(1).to_broadcast(bc), ALU.is_equal))
                        v(dve.tensor_tensor(hot, hot, topi[:, tt, half::2, :].unsqueeze(2).to_broadcast(bc), ALU.mult))
                        v(dve.tensor_reduce(pick[:, half], hot, AX_X, ALU.add))
                    v(dve.scalar_tensor_tensor(pick[:, 0], pick[:, 0], float(NKEYS), pick[:, 1], ALU.mult, ALU.add))
                    v(dve.tensor_copy(expert[:, tt].rearrange("p (h k) -> p h k", h=HEADS), pick[:, 0]))
                    dve.wait_ge(tk_exp, tt + 1)
                    v(dve.tensor_reduce(den[:, tt], prob[:, tt], AX_X, ALU.add))
                    v(dve.reciprocal(den[:, tt], den[:, tt]))
                    v(dve.tensor_tensor(prob[:, tt], prob[:, tt], den[:, tt].unsqueeze(2).to_broadcast([P, HEADS, TOPK]),
                                        ALU.mult))
                dve.wait_ge(gv_col, 24)
                v(dve.tensor_tensor(mod2[:, 0:48], psum[7][:, 0:48], vcol("b_mod_2", 0, 48), ALU.add))
                v(dve.scalar_tensor_tensor(gain[:, 2, :], mod2[:, 8:16], 1.0, vcol("g_mix_norm_2", 0, 8), ALU.add, ALU.mult))
                v(dve.scalar_tensor_tensor(gain[:, 3, :], mod2[:, 32:40], 1.0, vcol("g_ffn_norm_2", 0, 8), ALU.add, ALU.mult))

            @block.scalar
            def _(act):
                n = SLOTS["keys"][0]
                wait_slot(act, n)
                act.copy(keys, slot(n, NKEYS, NHP)).then_inc(keys_out, 1)
                act.wait_ge(keys_out, 1)
                act.sem_inc(slot_used[n % RING], 1)
                act.wait_ge(tk_best, 1)
                act.activation(prob[:, 0], best0[:, 0], ACT.Exp).then_inc(tk_exp, 1)
                for q in range(12, 24):
                    act_mod_row(act, q)
                act.wait_ge(tk_best, 2)
                act.activation(prob[:, 1], best0[:, 1], ACT.Exp).then_inc(tk_exp, 1)
        if STOP == "topk":
            return

        HALF = GRING
        BODY = 2 * HALF
        DIAGS = 4
        rows = area(10752, GRING, 2 * D)
        ROWS_AT = 10752
        prob2 = area(0, TT, NSEL)
        expert2 = area(256, TT, NSEL).bitcast(U32)
        stage = area(512, 2, HALF).bitcast(U32)
        pstage = area(528, BODY)
        hdot = area(544, BODY)
        hgel = area(560, BODY)
        zrow = area(576, 512)
        diag = area(1088, DIAGS, P)
        dump = area(1600, D)
        ptok = area(6144, TT, D)
        assert ROWS_AT + GRING * 2 * D <= ARENA and ROWS_AT >= 6144 + TT * D
        pe_copied = sem("pe_copied")
        row_loaded = [sem(f"row_loaded{j}") for j in range(GRING)]
        staged, pstaged, rows_used, dotted, gelued, diag_ready, z_ready, turn = (
            sem(x) for x in ("staged", "pstaged", "rows_used", "dotted", "gelued", "diag_ready", "z_ready", "turn"))
        px_ev, px_mm = sem("px_ev"), sem("px_mm")
        with nc.Block() as block:
            @block.vector
            def _(dve):
                dve.tensor_copy(prob2, prob.rearrange("p t h k -> p t (h k)"))
                dve.tensor_copy(expert2, expert)
        LOOPS = NSEL // BODY
        with nc.Block() as block:
            @block.gpsimd
            def _(pool):
                for tt in range(TT):
                    with pool.Fori(0, LOOPS) as i:
                        for half in range(2):
                            k = 2 * (tt * LOOPS) + half
                            pool.wait_ge(rows_used, i * BODY + (tt * NSEL + half * HALF + 1))
                            pool.tensor_copy(stage[:, half, :], expert2[:, tt, bass.ds(i * BODY + half * HALF, HALF)]
                                             ).then_inc(staged, 1)
                            pool.wait_ge(staged, i * 2 + (k + 1))
                            pool.sem_inc(turn, 1)
                            for j in range(HALF):
                                pool.wait_ge(rows_used, i * BODY + (tt * NSEL + half * HALF + j + 1))
                                pool.sem_inc(turn, 1)
                                pool.indirect_dma_start(rows[:, j, :], None, experts_in,
                                                        bass.IndirectOffsetOnAxis(ap=stage[:, half, j:j + 1], axis=0)
                                                        ).then_inc(row_loaded[j], 16)

            @block.vector
            def _(dve):
                v = chain("v", dve, seq_v)
                dve.memset(zrow, 0.0).then_inc(z_ready, 1)
                dve.sem_inc(diag_ready, 1)

                def make_diag(tt, i, q):
                    dve.wait_ge(gelued, i * BODY + (tt * NSEL + q + 1))
                    dve.wait_ge(rows_used, i * BODY + (tt * NSEL + q + GRING - DIAGS + 1))
                    dve.tensor_scalar(diag[:, q % DIAGS, :], ident, hgel[:, q:q + 1], pstage[:, q:q + 1],
                                      ALU.mult, ALU.mult).then_inc(diag_ready, 1)

                for tt in range(TT):
                    with dve.Fori(0, LOOPS) as i:
                        dve.wait_ge(diag_ready, i * BODY + (tt * NSEL + 1))
                        dve.tensor_copy(pstage, prob2[:, tt, bass.ds(i * BODY, BODY)]).then_inc(pstaged, 1)
                        dve.wait_ge(pstaged, i + (tt * LOOPS + 1))
                        for q in range(BODY):
                            dve.wait_ge(row_loaded[q % GRING], i * 32 + (tt * LOOPS * 32 + 16 * (q // GRING + 1)))
                            dve.tensor_tensor_reduce(dump, rows[:, q % GRING, 0:D], utok[:, tt, :], 1.0, 0.0,
                                                     ALU.mult, ALU.add, hdot[:, q:q + 1]).then_inc(dotted, 1)
                            if q:
                                make_diag(tt, i, q - 1)
                            dve.wait_ge(dotted, i * BODY + (tt * NSEL + q + 1))
                        make_diag(tt, i, BODY - 1)

            @block.scalar
            def _(act):
                for tt in range(TT):
                    with act.Fori(0, LOOPS) as i:
                        for q in range(BODY):
                            act.wait_ge(dotted, i * BODY + (tt * NSEL + q + 1))
                            act.activation(hgel[:, q:q + 1], hdot[:, q:q + 1], ACT.Gelu).then_inc(gelued, 1)

            @block.tensor
            def _(pe):
                pe.wait_ge(z_ready, 1)
                for b in range(2 * TT):
                    pe.matmul(psum[b][:, :], ident, zrow, start=True, stop=False, skip_group_check=True)
                pe.sem_inc(rows_used, GRING)
                for tt in range(TT):
                    with pe.Fori(0, LOOPS) as i:
                        for q in range(BODY):
                            pe.wait_ge(diag_ready, i * BODY + (tt * NSEL + q + 2))
                            for h in range(2):
                                ins = pe.matmul(psum[2 * tt + h][:, :], diag[:, q % DIAGS, :],
                                                rows[:, q % GRING, D + 512 * h:D + 512 * h + 512],
                                                start=False, stop=False, skip_group_check=True)
                            ins.then_inc(rows_used, 1)
        with nc.Block() as block:
            @block.scalar
            def _(act):
                for tt in range(TT):
                    for h in range(2):
                        act.copy(ptok[:, tt, 512 * h:512 * h + 512], psum[2 * tt + h][:, :]).then_inc(px_ev, 1)

            @block.tensor
            def _(pe):
                pe.wait_ge(px_ev, 2 * TT)
                for b in range(4):
                    for kk in range(2):
                        for tt in range(TT):
                            k = 2 * b + kk
                            ins = pe.transpose(psum[4 + b][:, kk * T + tt * P:kk * T + (tt + 1) * P],
                                               ptok[:, tt, k * P:(k + 1) * P], ident)
                    ins.then_inc(px_mm, 1)

            @block.vector
            def _(dve):
                for k in range(KT):
                    dve.wait_ge(px_mm, k // 2 + 1)
                    dve.scalar_tensor_tensor(xT[:, k, :], psum[4 + k // 2][:, (k % 2) * T:(k % 2 + 1) * T],
                                             mod1[:, 40 + k:41 + k], xT[:, k, :], ALU.mult, ALU.add)
        if STOP == "peer":
            return

        norm_block("fin", vcol("final_g", 0, 8), None, uT)
        with nc.Block() as block:
            @block.scalar
            def _(act):
                act.copy(xT[:, :, :], uT[:, :, :])
        norm_block("mix2", gain[:, 2, :], mod2[:, 0:8], uT)

        qk = area(0, 16, T)
        qki = area(4096, 5, T)
        vtok = area(5376, 2, TT, CH)
        sgate = area(7424, 2 * KT, T)
        wi = area(11520, TT, HEADS)
        IDX_SCALE = (8 ** -0.5) * (64 ** -0.5)
        full = slice(0, P)

        def item(kind, s, col, dst, func=ACT.Copy, scale=1.0):
            return kind, s, col, dst, func, scale
        items = [item("feat", 0, i * P, qk[:, i, :]) for i in range(4)]
        items += [item("feat", 1, i * P, qk[:, 4 + i, :]) for i in range(4)]
        items += [item("token", 2, tt, vtok[:, 0, tt, :]) for tt in range(TT)]
        items += [item("feat", 3, i * P, qki[:, i, :]) for i in range(4)]
        items += [item("key", 4, 0, qki[:, 4, :])]
        items += [item("weight", 4, tt, wi[:, tt, :], scale=IDX_SCALE) for tt in range(TT)]
        items += [item("feat", 5, i * P, qk[:, 8 + i, :]) for i in range(4)]
        items += [item("feat", 6, i * P, qk[:, 12 + i, :]) for i in range(4)]
        items += [item("token", 7, tt, vtok[:, 1, tt, :]) for tt in range(TT)]
        items += [item("feat", 8 + i // 4, (i % 4) * P, sgate[:, i, :], ACT.Sigmoid) for i in range(16)]
        i2_mm, i2_ev = sem("i2_mm"), sem("i2_ev")
        with nc.Block() as block:
            @block.sync
            def _(sp):
                load_slots(sp, after("mod2"), after("w_in2"))

            @block.tensor
            def _(pe):
                s0 = SLOTS["w_in2"][0]
                for n, (kind, s, col, *_) in enumerate(items):
                    if n == 0 or items[n - 1][1] != s:
                        wait_slot(pe, s0 + s)
                    if n >= 8:
                        pe.wait_ge(i2_ev, n - 7)
                    bank, w = psum[n % 8], slot(s0 + s)
                    for half in range(2 if kind == "key" else 1):
                        for k in range(KT):
                            if kind == "feat":
                                o, l, r = bank[:, 0:T], w[:, k, col:col + P], uT[:, k, :]
                            elif kind == "key":
                                o, l, r = bank[64 * half:64 * half + 64, 0:T], w[:, k, 0:64], uT[:, k, :]
                            elif kind == "token":
                                o, l, r = bank[:, :], uT[:, k, col * P:(col + 1) * P], w[:, k, :]
                            else:
                                o, l, r = bank[:, 0:HEADS], uT[:, k, col * P:(col + 1) * P], w[:, k, 64:64 + HEADS]
                            ins = pe.matmul(o, l, r, start=(k == 0), stop=(k == KT - 1))
                    ins.then_inc(i2_mm, 1)

            @block.scalar
            def _(act):
                s0 = SLOTS["w_in2"][0]
                for n, (kind, s, col, dst, func, scale) in enumerate(items):
                    act.wait_ge(i2_mm, n + 1)
                    if n == len(items) - 1 or items[n + 1][1] != s:
                        act.sem_inc(slot_used[(s0 + s) % RING], 1)
                    width = {"feat": T, "key": T, "token": CH, "weight": HEADS}[kind]
                    act.activation(dst, psum[n % 8][:, 0:width], func, scale=scale).then_inc(i2_ev, 1)
        if STOP == "w_in2":
            return

        rope = slot(SLOTS["rope"][0], P, 32).rearrange("p k n -> p (k n)")
        cos, sin = (rope[:, 0:T], rope[:, 512:512 + T]), (rope[:, T:512], rope[:, 512 + T:1024])
        causal = rope[:, 1024:1536].rearrange("p (t s) -> p t s", t=TT)
        rot = (rope[:, 1536:1664], rope[:, 1664:1792])
        rs = area(11552, 16, T)
        ro = area(15648, 4, 2, T)
        GROUPS = 19
        hr = {x: sem("hr_" + x) for x in ("sq", "mm", "iev", "sev", "rec", "nrm", "cs", "rev", "fin")}
        gains2 = ("g_q_dsa_2", "g_k_dsa_2", "g_q_moba_2", "g_k_moba_2")
        with nc.Block() as block:
            @block.tensor
            def _(pe):
                wait_slot(pe, SLOTS["rope"][0])
                for g in range(GROUPS):
                    bank = psum[g % 8]
                    if 8 <= g < 11:
                        pe.wait_ge(hr["iev"], g - 7)
                    if g >= 11:
                        pe.wait_ge(hr["sev"], g - 10)
                        pe.wait_ge(hr["nrm"], 2 * (g - 11) + 2)
                    if 3 <= g < 11:
                        pe.wait_ge(hr["sq"], (g - 3) // 2 + 1)
                    for j in range(2):
                        if g < 3:
                            if 2 * g + j == 5:
                                continue
                            l, r = rot[1], qki[:, 2 * g + j, :]
                        elif g < 11:
                            l, r = ones, rs[:, 2 * (g - 3) + j, :]
                        else:
                            l, r = rot[0], qk[:, 2 * (g - 11) + j, :]
                        ins = pe.matmul(bank[:, j * T:(j + 1) * T], l, r, start=True, stop=True)
                    ins.then_inc(hr["mm"], 1)

            @block.scalar
            def _(act):
                for i in range(4):
                    act.activation(rs[:, 4 * i:4 * i + 4, :], qk[:, 4 * i:4 * i + 4, :], ACT.Square).then_inc(hr["sq"], 1)
                for g in range(3, 11):
                    act.wait_ge(hr["mm"], g + 1)
                    act.activation(rs[:, 2 * g - 6:2 * g - 4, :], psum[g % 8][:, :].rearrange("p (j t) -> p j t", j=2),
                                   ACT.Sqrt, bias=epsc[:, 0:1], scale=1.0 / HD).then_inc(hr["sev"], 1)

            @block.vector
            def _(dve):
                wait_slot(dve, SLOTS["rope"][0])
                v = chain("v", dve, seq_v)

                def rotate(g, x, n, which, base):
                    dve.wait_ge(hr["mm"], g + 1)
                    t = ro[:, g % 4, 0:n, :]
                    s = [P, n, T]
                    ps = psum[g % 8][:, 0:n * T].rearrange("p (j t) -> p j t", j=n)
                    v(dve.tensor_tensor(t, ps, sin[which].unsqueeze(1).to_broadcast(s), ALU.mult))
                    dve.sem_inc(hr[base], 1)
                    v(dve.tensor_tensor(x, x, cos[which].unsqueeze(1).to_broadcast(s), ALU.mult))
                    dve.tensor_tensor(x, x, t, ALU.add).then_inc(hr["fin"], 1)

                for g in range(3):
                    n = 1 if g == 2 else 2
                    rotate(g, qki[:, 2 * g:2 * g + n, :], n, 1, "iev")
                for i in range(8):
                    dve.wait_ge(hr["sev"], i + 1)
                    v(dve.reciprocal(rs[:, 2 * i:2 * i + 2, :], rs[:, 2 * i:2 * i + 2, :]))
                    for j in (2 * i, 2 * i + 1):
                        dve.scalar_tensor_tensor(qk[:, j, :], qk[:, j, :], vcol(gains2[j // 4]), rs[:, j, :],
                                                 ALU.mult, ALU.mult).then_inc(hr["nrm"], 1)
                for i in range(8):
                    rotate(11 + i, qk[:, 2 * i:2 * i + 2, :], 2, 0, "rev")
        if STOP == "rope":
            return

        relu = area(0 + 15648, 4, T)
        score = area(16672, TT, T)
        left = area(17184, TT, T)
        max8 = area(17696, TT, 8)
        maskd = area(17712, TT, T)
        ix_mm, ix_relu, ix_acc, ix_top = sem("ix_mm"), sem("ix_relu"), sem("ix_acc"), sem("ix_top")
        width = [P * (tt + 1) for tt in range(TT)]
        with nc.Block() as block:
            @block.tensor
            def _(pe):
                for n in range(TT * HEADS):
                    tt, h = n // HEADS, n % HEADS
                    s = slice(64 * (h % 2), 64 * (h % 2) + 64)
                    if n >= 8:
                        pe.wait_ge(ix_relu, n - 7)
                    pe.matmul(psum[n % 8][:, 0:width[tt]], qki[s, h // 2, tt * P:(tt + 1) * P],
                              qki[s, 4, 0:width[tt]], start=True, stop=True).then_inc(ix_mm, 1)

            @block.scalar
            def _(act):
                for n in range(TT * HEADS):
                    tt = n // HEADS
                    act.wait_ge(ix_mm, n + 1)
                    if n >= 4:
                        act.wait_ge(ix_acc, n - 3)
                    act.activation(relu[:, n % 4, 0:width[tt]], psum[n % 8][:, 0:width[tt]],
                                   ACT.Relu).then_inc(ix_relu, 1)

            @block.vector
            def _(dve):
                for n in range(TT * HEADS):
                    tt, h = n // HEADS, n % HEADS
                    dve.wait_ge(ix_relu, n + 1)
                    if h:
                        dve.wait_ge(ix_acc, n)
                    dst = score[:, tt, 0:width[tt]]
                    prev = causal[:, tt, 0:width[tt]] if h == 0 else dst
                    dve.scalar_tensor_tensor(dst, relu[:, n % 4, 0:width[tt]], wi[:, tt, h:h + 1], prev,
                                             ALU.mult, ALU.add).then_inc(ix_acc, 1)
                dve.wait_ge(ix_acc, TT * HEADS)
                count = 0
                for r in range(DSA_TOPK // 8):
                    for op in range(2):
                        for tt in range(TT):
                            src = score if r == 0 else left
                            if r or op:
                                dve.wait_ge(ix_top, count - TT + 1)
                            if op == 0:
                                ins = dve.max(max8[:, tt, :], src[:, tt, 0:width[tt]])
                            else:
                                ins = dve.match_replace(left[:, tt, 0:width[tt]], max8[:, tt, :],
                                                        src[:, tt, 0:width[tt]], TAKEN)
                            ins.then_inc(ix_top, 1)
                            count += 1
                v = chain("v", dve, seq_v)
                dve.wait_ge(ix_top, count)
                for tt in range(TT):
                    w = slice(0, width[tt])
                    v(dve.tensor_scalar(maskd[:, tt, w], left[:, tt, w], TAKEN / 2, NEG, ALU.is_gt, ALU.mult))
                    v(dve.tensor_tensor(maskd[:, tt, w], maskd[:, tt, w], causal[:, tt, w], ALU.add))
        if STOP == "idx":
            return

        NI = 16
        sm = area(18224, 4, T)
        pT = area(19248, 2, T)
        nmax, psm, rsm = area(19760, NI), area(19776, NI), area(19792, NI)
        at = {x: sem("at_" + x) for x in ("s", "sm", "max", "exp", "rec", "p", "t", "pT", "o", "oT")}

        def what(n):
            b, h, tt = n // 8, n // 2 % 4, n % 2
            return b, h, tt, width[tt]
        with nc.Block() as block:
            @block.sync
            def _(sp):
                load_slots(sp, after("w_in2"), after("rope"))

            @block.tensor
            def _(pe):
                def scores(n):
                    b, h, tt, w = what(n)
                    if n >= 4:
                        pe.wait_ge(at["sm"], n - 3)
                    pe.matmul(psum[n % 4][:, 0:w], qk[:, 8 * b + h, tt * P:(tt + 1) * P], qk[:, 8 * b + 4 + h, 0:w],
                              start=True, stop=True).then_inc(at["s"], 1)

                def flips(n):
                    b, h, tt, w = what(n)
                    pe.wait_ge(at["p"], n + 1)
                    if n >= 2:
                        pe.wait_ge(at["pT"], n - 1)
                    for st_ in range(tt + 1):
                        ins = pe.transpose(psum[4 + n % 2][:, st_ * P:(st_ + 1) * P],
                                           sm[:, n % 4, st_ * P:(st_ + 1) * P], ident)
                    ins.then_inc(at["t"], 1)

                def values(n):
                    b, h, tt, w = what(n)
                    pe.wait_ge(at["pT"], n + 1)
                    if n >= 2:
                        pe.wait_ge(at["oT"], n - 1)
                    for st_ in range(tt + 1):
                        ins = pe.matmul(psum[6 + n % 2][:, 0:P], vtok[:, b, st_, h * HD:(h + 1) * HD],
                                        pT[:, n % 2, st_ * P:(st_ + 1) * P], start=(st_ == 0), stop=(st_ == tt))
                    ins.then_inc(at["o"], 1)
                for n in range(NI + 3):
                    if n < NI:
                        scores(n)
                    if 2 <= n < NI + 2:
                        flips(n - 2)
                    if n >= 3:
                        values(n - 3)

            @block.vector
            def _(dve):
                for n in range(NI + 1):
                    if n < NI:
                        b, h, tt, w = what(n)
                        dve.wait_ge(at["s"], n + 1)
                        if n >= 4:
                            dve.wait_ge(at["t"], n - 3)
                        mask = (causal if b else maskd)[:, tt, 0:w]
                        dve.scalar_tensor_tensor(sm[:, n % 4, 0:w], psum[n % 4][:, 0:w], HD ** -0.5, mask,
                                                 ALU.mult, ALU.add).then_inc(at["sm"], 1)
                        dve.wait_ge(at["sm"], n + 1)
                        dve.tensor_reduce(nmax[:, n:n + 1], sm[:, n % 4, 0:w], AX_X, ALU.max,
                                          negate=True).then_inc(at["max"], 1)
                    if n:
                        m, w = n - 1, what(n - 1)[3]
                        dve.wait_ge(at["exp"], m + 1)
                        dve.reciprocal(rsm[:, m:m + 1], psm[:, m:m + 1]).then_inc(at["rec"], 1)
                        dve.wait_ge(at["rec"], m + 1)
                        dve.tensor_scalar(sm[:, m % 4, 0:w], sm[:, m % 4, 0:w], rsm[:, m:m + 1], None,
                                          ALU.mult).then_inc(at["p"], 1)
                dve.sem_inc(slot_used[SLOTS["rope"][0] % RING], 1)

            @block.scalar
            def _(act):
                for n in range(NI + 3):
                    if n < NI:
                        b, h, tt, w = what(n)
                        act.wait_ge(at["max"], n + 1)
                        act.activation(sm[:, n % 4, 0:w], sm[:, n % 4, 0:w], ACT.Exp, bias=nmax[:, n:n + 1],
                                       accum_out=psm[:, n:n + 1]).then_inc(at["exp"], 1)
                    if 2 <= n < NI + 2:
                        m, w = n - 2, what(n - 2)[3]
                        act.wait_ge(at["t"], m + 1)
                        if m >= 2:
                            act.wait_ge(at["o"], m - 1)
                        act.copy(pT[:, m % 2, 0:w], psum[4 + m % 2][:, 0:w]).then_inc(at["pT"], 1)
                    if n >= 3:
                        b, h, tt, w = what(n - 3)
                        act.wait_ge(at["o"], n - 2)
                        act.copy(mixT[:, 4 * b + h, tt * P:(tt + 1) * P], psum[6 + (n - 3) % 2][:, 0:P]).then_inc(at["oT"], 1)
        if STOP == "attn":
            return

        merged = area(15648, KT, T)
        gated = area(17696, 4, T)
        br_mm, br_ev, br_t = sem("br_mm"), sem("br_ev"), sem("br_t")
        with nc.Block() as block:
            @block.sync
            def _(sp):
                load_slots(sp, after("rope"), after("w_br"))

            @block.tensor
            def _(pe):
                s0 = SLOTS["w_br"][0]
                for n in range(16):
                    b, m = n // 8, n % 8
                    if m == 0:
                        wait_slot(pe, s0 + b)
                    if n >= 8:
                        pe.wait_ge(br_ev, n - 7)
                    for k in range(4):
                        ins = pe.matmul(psum[n % 8][:, 0:T], slot(s0 + b, D, 4)[:, k, m * P:(m + 1) * P],
                                        mixT[:, 4 * b + k, :], start=(k == 0), stop=(k == 3))
                    ins.then_inc(br_mm, 1)

            @block.vector
            def _(dve):
                s0 = SLOTS["w_br"][0]
                for n in range(16):
                    b, m = n // 8, n % 8
                    dve.wait_ge(br_mm, n + 1)
                    if m == 7:
                        dve.sem_inc(slot_used[(s0 + b) % RING], 1)
                    dst = gated[:, m % 4, :] if b else merged[:, m, :]
                    if b and m >= 4:
                        dve.wait_ge(br_t, m - 3)
                    dve.tensor_tensor(dst, psum[n % 8][:, 0:T], sgate[:, n, :], ALU.mult).then_inc(br_ev, 1)
                    if b:
                        dve.wait_ge(br_ev, n + 1)
                        dve.tensor_tensor(merged[:, m, :], merged[:, m, :], dst, ALU.add).then_inc(br_t, 1)
        if STOP == "merged":
            return
        residual_block("o2", "w_out2", eight, merged, mod2[:, 16:24], (after("w_br"), after("w_out2")))
        norm_block("ffn2", gain[:, 3, :], mod2[:, 24:32], uT)
        ff = area(0, FT, T)
        gu_mm, gu_act, gu_ev = sem("gu_mm"), sem("gu_act"), sem("gu_ev")
        NGU = SLOTS["w_gu"][1]
        with nc.Block() as block:
            @block.sync
            def _(sp):
                load_slots(sp, after("w_out2"), after("w_gu"))

            @block.tensor
            def _(pe):
                s0 = SLOTS["w_gu"][0]
                for n in range(4 * NGU):
                    s, j = n // 4, n % 4
                    if j == 0:
                        wait_slot(pe, s0 + s)
                    if s >= 2:
                        if j < 2:
                            pe.wait_ge(gu_act, 2 * (s - 2) + j + 1)
                        else:
                            pe.wait_ge(gu_ev, 2 * (s - 2) + j - 1)
                    for k in range(KT):
                        ins = pe.matmul(psum[n % 8][:, 0:T], slot(s0 + s)[:, k, j * P:(j + 1) * P], uT[:, k, :],
                                        start=(k == 0), stop=(k == KT - 1))
                    ins.then_inc(gu_mm, 1)

            @block.scalar
            def _(act):
                for n in range(2 * NGU):
                    s, j = n // 2, n % 2
                    act.wait_ge(gu_mm, 4 * s + j + 1)
                    act.activation(ff[:, n, :], psum[(4 * s + j) % 8][:, 0:T], ACT.Silu).then_inc(gu_act, 1)

            @block.vector
            def _(dve):
                for n in range(2 * NGU):
                    s, j = n // 2, n % 2
                    dve.wait_ge(gu_mm, 4 * s + j + 3)
                    dve.wait_ge(gu_act, n + 1)
                    dve.tensor_tensor(ff[:, n, :], ff[:, n, :], psum[(4 * s + 2 + j) % 8][:, 0:T],
                                      ALU.mult).then_inc(gu_ev, 1)
                    if j == 1:
                        dve.sem_inc(slot_used[(SLOTS["w_gu"][0] + s) % RING], 1)
        residual_block("dn", "w_down", [(i, 0) for i in range(8)], ff, mod2[:, 40:48],
                       (after("w_gu"), NSLOTS), width=P, kts=FT)
        out_done = sem("out_done")
        with nc.Block() as block:
            @block.sync
            def _(sp):
                sp.dma_start(out, xT[:]).then_inc(out_done, 16)
                sp.wait_ge(out_done, 16)

STOP = None


def kernel(**inputs):
    import concourse.bacc as bacc
    from concourse.bass_utils import run_bass_kernel_spmd

    w = {k: np.asarray(v) for k, v in inputs.items()}

    def cols(a):
        return np.asarray(a).reshape(-1, P).T

    vecs = np.ascontiguousarray(np.concatenate([cols(w[name]) for name, _ in VECS], axis=1))

    slots = np.zeros((NSLOTS, P, SLOT), np.float32)

    def tiles(n, a):
        k = a.shape[0] // P
        slots[n, :, 0:k * a.shape[1]] = a.reshape(k, P, -1).transpose(1, 0, 2).reshape(P, -1)

    def fill(name, a, width=512):
        s0, n = SLOTS[name]
        for s in range(n):
            tiles(s0 + s, a[:, s * width:(s + 1) * width])

    fill("ada", w["ada_w"][0])
    fill("ada2", w["ada_w"][0][:, 2048:])
    fill("ada3", w["ada_w"][0][:, 3072:])
    fill("w_in", w["w_in"][0][:, :2560])
    wi = w["w_in"][0][:, 2560:]
    tiles(SLOTS["w_in"][0] + 5, np.concatenate([wi, np.zeros((D, 256), np.float32)], axis=1))
    s = SLOTS["lora"][0]
    slots[s, 0:64, 0:CH] = w["rwkv_w2"][0]
    slots[s, 64:128, 0:CH] = w["rwkv_a2"][0]
    slots[s, :, CH:2 * CH] = w["rwkv_g2"][0]
    fill("mod2", w["w_mod_2"][0])
    fill("w_out", w["w_out"][0])
    fill("w_q", w["peer_w_q"][0])
    slots[SLOTS["keys"][0], :, 0:2048] = w["peer_sub_keys"][0].reshape(16, NKEYS, P).transpose(2, 0, 1).reshape(P, -1)
    wi = w["w_in_2"][0]
    s = SLOTS["w_in2"][0]
    for j in range(4):
        tiles(s + j, wi[:, j * 512:(j + 1) * 512])
    tiles(s + 4, np.concatenate([wi[:, 2048:2120], np.zeros((D, 440), np.float32)], axis=1))
    for j in range(7):
        tiles(s + 5 + j, wi[:, 2120 + j * 512:2120 + (j + 1) * 512])
    consts, rope = shape_constants()
    slots[SLOTS["rope"][0]] = rope
    tiles(SLOTS["w_br"][0], w["w_br_dsa_2"][0])
    tiles(SLOTS["w_br"][0] + 1, w["w_br_moba_2"][0])
    fill("w_out2", w["w_out_2"][0])
    gu = w["w_gate_up_2"][0]
    for j in range(11):
        tiles(SLOTS["w_gu"][0] + j, np.concatenate([gu[:, j * 256:(j + 1) * 256],
                                                    gu[:, FF + j * 256:FF + (j + 1) * 256]], axis=1))
    fill("w_down", w["w_down_2"][0], P)
    experts = np.concatenate([w["peer_u"][0], w["peer_v"][0]], axis=1)
    xT = np.ascontiguousarray(w["x"][0].T.reshape(KT, P, T).transpose(1, 0, 2))

    nc = bacc.Bacc("TRN2", target_bir_lowering=False, num_devices=1)
    arrays = {"xT_in": xT, "vecs_in": vecs, "consts_in": consts, "slots_in": slots, "experts_in": experts}
    args = [nc.dram_tensor(k, a.shape, mybir.dt.from_np(a.dtype), kind="ExternalInput").ap()
            for k, a in arrays.items()]
    out = nc.dram_tensor("out_dram", (P, KT, T), F32, kind="ExternalOutput").ap()
    build(nc, *args, out)
    r = run_bass_kernel_spmd(nc, [arrays], core_ids=[0])
    o = r.results[0]["out_dram"]
    return np.ascontiguousarray(o.transpose(1, 0, 2).reshape(D, T).T).reshape(1, T, D)
```
